# Optimizing a Trainium2 kernel written in Bass

```python
import jax, jax.numpy as jnp
from jax import lax
import numpy as np

D_MODEL = 1024
BATCH = 1
SEQ = 256
DEPTH = 1

N_RET_HEADS = 8
RET_HEAD_DIM = D_MODEL // N_RET_HEADS
RET_WIDTH = N_RET_HEADS * RET_HEAD_DIM
RET_CHUNK = 128
ROPE_BASE = 10000.0
CONV_WIDTH = D_MODEL
CONV_GROUPS = 8
CONV_K = 3
FFN_HIDDEN = -(-8 * D_MODEL // (3 * 256)) * 256
EPS = 1e-6
N_MOD = 6
IN_SPLITS = [RET_WIDTH, RET_WIDTH, RET_WIDTH, RET_WIDTH,
             CONV_WIDTH, CONV_WIDTH, CONV_WIDTH,
             D_MODEL, D_MODEL]
IN_COLS = sum(IN_SPLITS)


def rmsnorm(x, g):
    xf = x.astype(jnp.float32)
    y = xf * lax.rsqrt(jnp.mean(xf * xf, axis=-1, keepdims=True) + EPS)
    return (y * g.astype(jnp.float32)).astype(x.dtype)

def head_layernorm(y):
    yf = y.astype(jnp.float32)
    mu = jnp.mean(yf, axis=-1, keepdims=True)
    var = jnp.mean((yf - mu) ** 2, axis=-1, keepdims=True)
    return ((yf - mu) * lax.rsqrt(var + EPS)).astype(y.dtype)

def modulate(h, shift, scale):
    return h * (1.0 + scale[:, None, :]) + shift[:, None, :]

def rope(t, cos, sin):
    t1, t2 = jnp.split(t, 2, axis=-1)
    out = jnp.concatenate([t1 * cos - t2 * sin, t1 * sin + t2 * cos], axis=-1)
    return out.astype(t.dtype)

def retention_chunkwise(q, k, v, log_gamma):
    B, S, H, d = q.shape
    N = S // RET_CHUNK

    def to_chunks(t):
        return t.reshape(B, N, RET_CHUNK, H, t.shape[-1]).transpose(0, 3, 1, 2, 4)

    qc, kc, vc = to_chunks(q), to_chunks(k), to_chunks(v)
    idx = jnp.arange(RET_CHUNK, dtype=jnp.float32)
    rel = idx[:, None] - idx[None, :]
    lg = log_gamma[:, None, None]
    dmask = jnp.where(rel >= 0, jnp.exp(lg * jnp.maximum(rel, 0.0)), 0.0)
    scores = jnp.einsum('bhncd,bhnmd->bhncm', qc, kc) * dmask[None, :, None]
    inner = jnp.einsum('bhncm,bhnme->bhnce', scores, vc)
    zeta = jnp.exp(log_gamma[:, None] * (RET_CHUNK - 1 - idx)[None, :])
    kv = jnp.einsum('bhncd,bhnce->bhnde', kc * zeta[None, :, None, :, None], vc)
    chunk_decay = jnp.exp(log_gamma * RET_CHUNK)[None, :, None, None]

    def step(R, kv_n):
        return R * chunk_decay + kv_n, R

    _, R_prev = lax.scan(step, jnp.zeros_like(kv[:, :, 0]), kv.transpose(2, 0, 1, 3, 4))
    R_prev = R_prev.transpose(1, 2, 0, 3, 4)
    xi = jnp.exp(log_gamma[:, None] * (idx + 1.0)[None, :])
    cross = jnp.einsum('bhncd,bhnde->bhnce', qc, R_prev) * xi[None, :, None, :, None]
    out = inner + cross
    return out.transpose(0, 2, 3, 1, 4).reshape(B, S, H, vc.shape[-1])

def first_inputs(seed: int = 0) -> dict:
    key = jax.random.key(seed)
    ks = jax.random.split(key, 20)
    D = D_MODEL
    nrm = lambda k, shape, fan_in, s=1.0: s * jax.random.normal(k, shape, jnp.float32) * fan_in ** -0.5
    x = jax.random.normal(ks[0], (BATCH, SEQ, D), jnp.float32)
    c = jax.random.normal(ks[1], (BATCH, D), jnp.float32)
    positions = jnp.broadcast_to(jnp.arange(SEQ, dtype=jnp.int32)[None, :], (BATCH, SEQ))
    return {
        "x": x,
        "c": c,
        "positions": positions,
        "ada_w": nrm(ks[2], (DEPTH, D, N_MOD * D), D, 0.1),
        "ada_b": 0.02 * jax.random.normal(ks[3], (DEPTH, N_MOD * D), jnp.float32),
        "norm_mix_g": 1.0 + 0.02 * jax.random.normal(ks[4], (DEPTH, D), jnp.float32),
        "w_in": nrm(ks[5], (DEPTH, D, IN_COLS), D),
        "conv_w": nrm(ks[6], (DEPTH, CONV_K, CONV_WIDTH), CONV_K),
        "ret_w_out": nrm(ks[7], (DEPTH, RET_WIDTH, D), RET_WIDTH),
        "conv_w_out": nrm(ks[8], (DEPTH, CONV_WIDTH, D), CONV_WIDTH),
        "mix_w_out": nrm(ks[9], (DEPTH, D, D), D),
        "norm_ffn_g": 1.0 + 0.02 * jax.random.normal(ks[10], (DEPTH, D), jnp.float32),
        "ffn_w_gate": nrm(ks[11], (DEPTH, D, FFN_HIDDEN), D),
        "ffn_w_up": nrm(ks[12], (DEPTH, D, FFN_HIDDEN), D),
        "ffn_w_down": nrm(ks[13], (DEPTH, FFN_HIDDEN, D), FFN_HIDDEN),
        "final_norm_g": 1.0 + 0.02 * jax.random.normal(ks[14], (D,), jnp.float32),
    }

def first_block(x, c, positions, ada_w, ada_b, norm_mix_g, w_in, conv_w, ret_w_out,
              conv_w_out, mix_w_out, norm_ffn_g, ffn_w_gate, ffn_w_up, ffn_w_down,
              final_norm_g):
    B, S, D = x.shape
    H, d = N_RET_HEADS, RET_HEAD_DIM
    log_gamma = jnp.log(1.0 - 2.0 ** (-5.0 - jnp.arange(H, dtype=jnp.float32)))
    inv_freq = 1.0 / (ROPE_BASE ** (jnp.arange(0, d, 2, dtype=jnp.float32) / d))
    ang = positions.astype(jnp.float32)[..., None] * inv_freq
    cos, sin = jnp.cos(ang)[:, :, None, :], jnp.sin(ang)[:, :, None, :]
    split_pts = list(np.cumsum(IN_SPLITS)[:-1])
    cs = jax.nn.silu(c)

    for l in range(DEPTH):
        mod = cs @ ada_w[l] + ada_b[l]
        sh_m, sc_m, gt_m, sh_f, sc_f, gt_f = jnp.split(mod, N_MOD, axis=-1)

        h = modulate(rmsnorm(x, norm_mix_g[l]), sh_m, sc_m)
        proj = h @ w_in[l]
        q, k, v, g_ret, b_cv, c_cv, u_cv, g_a, g_b = jnp.split(proj, split_pts, axis=-1)

        q = rope(q.reshape(B, S, H, d), cos, sin)
        k = rope(k.reshape(B, S, H, d), cos, sin) * (d ** -0.5)
        v = v.reshape(B, S, H, d)
        y_ret = head_layernorm(retention_chunkwise(q, k, v, log_gamma)).reshape(B, S, RET_WIDTH)
        y_a = (jax.nn.silu(g_ret) * y_ret) @ ret_w_out[l]

        u = c_cv * u_cv
        u_pad = jnp.pad(u, ((0, 0), (CONV_K - 1, 0), (0, 0)))
        w = conv_w[l]
        conv = u_pad[:, 0:S] * w[0]
        for tap in range(1, CONV_K):
            conv = conv + u_pad[:, tap:tap + S] * w[tap]
        y_b = (b_cv * conv) @ conv_w_out[l]

        merged = jax.nn.sigmoid(g_a) * y_a + jax.nn.sigmoid(g_b) * y_b
        x = x + gt_m[:, None, :] * (merged @ mix_w_out[l])

        h = modulate(rmsnorm(x, norm_ffn_g[l]), sh_f, sc_f)
        f = (jax.nn.silu(h @ ffn_w_gate[l]) * (h @ ffn_w_up[l])) @ ffn_w_down[l]
        x = x + gt_f[:, None, :] * f

    return rmsnorm(x, final_norm_g)


DEPTH_2 = 2

CHUNK = 64
N_MIXERS = 2
N_RWKV = (DEPTH_2 + 1) // 2
N_MLSTM = DEPTH_2 // 2
NEG = -1e30

RW_HEAD = 64
RW_HEADS = D_MODEL // RW_HEAD
LORA_W = 64
LORA_A = 64
LORA_G = 160
RW_SEGS = (D_MODEL, LORA_W, D_MODEL, D_MODEL, LORA_A, LORA_G)
RW_IN = sum(RW_SEGS)
GN_EPS = 64e-5

ML_HEADS = 8
ML_QK = D_MODEL // 2 // ML_HEADS
ML_V = D_MODEL // ML_HEADS
ML_QKW = 2 * ML_HEADS * ML_QK
ML_VW = ML_HEADS * ML_V
ML_IN = ML_QKW + 2 * ML_VW + 2 * ML_HEADS
CONV_W = 4
GATE_CAP = 15.0

D_FF = -(-(8 * D_MODEL) // (3 * 256)) * 256


def _rms(x):
    xf = x.astype(jnp.float32)
    return (xf * lax.rsqrt(jnp.mean(xf * xf, -1, keepdims=True) + EPS)).astype(x.dtype)

def _softcap(t):
    return GATE_CAP * jnp.tanh(t / GATE_CAP)

def _token_shift(x):
    return jnp.pad(x[:, :-1], ((0, 0), (1, 0), (0, 0)))

def _rwkv7_step(state, inp):
    r_t, w_t, k_t, v_t, a_t, b_t = inp
    sa = jnp.einsum('bhvk,bhk->bhv', state, a_t)
    state = state * w_t[:, :, None, :] + sa[..., None] * b_t[:, :, None, :] + v_t[..., None] * k_t[:, :, None, :]
    y = jnp.einsum('bhvk,bhk->bhv', state, r_t)
    return state, y

def _rwkv7_mix(x, mix, w_in, w0, w2, a0, a2, g2, k_k, k_a, r_k, gn_w, gn_b, w_out):
    B, S, D = x.shape
    xx = _token_shift(x) - x
    xs = x[None] + xx[None] * mix[:, None, None, :]
    outs = []
    off = 0
    for i, n in enumerate(RW_SEGS):
        outs.append(xs[i] @ w_in[:, off:off + n])
        off += n
    r, wl, k, v, al, gl = outs
    w_log = -jax.nn.softplus(-(w0 + jnp.tanh(wl) @ w2)) - 0.5
    decay = jnp.exp(-jnp.exp(w_log.astype(jnp.float32)))
    a = jax.nn.sigmoid(a0 + al @ a2)
    g = jax.nn.sigmoid(gl) @ g2
    hs = lambda t: t.reshape(B, S, RW_HEADS, RW_HEAD).astype(jnp.float32)
    kk = hs(k * k_k)
    kk = kk / jnp.maximum(jnp.linalg.norm(kk, axis=-1, keepdims=True), 1e-12)
    k = k * (1.0 + (a - 1.0) * k_a)
    rh, kh, vh, ah, wh = hs(r), hs(k), hs(v), hs(a), hs(decay)
    tm = lambda t: jnp.moveaxis(t, 1, 0)
    state0 = jnp.zeros((B, RW_HEADS, RW_HEAD, RW_HEAD), jnp.float32)
    _, y = lax.scan(_rwkv7_step, state0, (tm(rh), tm(wh), tm(kh), tm(vh), tm(-kk), tm(kk * ah)))
    y = jnp.moveaxis(y, 0, 1)
    mu = jnp.mean(y, -1, keepdims=True)
    var = jnp.mean(jnp.square(y - mu), -1, keepdims=True)
    y = ((y - mu) * lax.rsqrt(var + GN_EPS)).reshape(B, S, D) * gn_w + gn_b
    bonus = (jnp.sum(rh * kh * r_k, -1, keepdims=True) * vh).reshape(B, S, D)
    return ((y + bonus).astype(x.dtype) * g) @ w_out

def _causal_dwconv(x, w, b):
    y = lax.conv_general_dilated(x, w[:, None, :], window_strides=(1,), padding=[(CONV_W - 1, 0)],
                                 dimension_numbers=('NWC', 'WIO', 'NWC'), feature_group_count=x.shape[-1])
    return y + b

def _mlstm_chunk_step(carry, inp):
    C, n, m = carry
    g_c, m_l, C_l, n_l = inp
    m_new = jnp.maximum(g_c + m, m_l)
    sa = jnp.exp(g_c + m - m_new)
    sb = jnp.exp(m_l - m_new)
    C_new = sa[..., None, None] * C + sb[..., None, None] * C_l
    n_new = sa[..., None] * n + sb[..., None] * n_l
    return (C_new, n_new, m_new), (C, n, m)

def _mlstm_mix(x, w_in, conv_w, conv_b, b_i, b_f, hn_w, w_out):
    B, S, D = x.shape
    NC = S // CHUNK
    p = x @ w_in
    qk = jax.nn.silu(_causal_dwconv(p[..., :ML_QKW], conv_w, conv_b))
    v = p[..., ML_QKW:ML_QKW + ML_VW]
    o = p[..., ML_QKW + ML_VW:ML_QKW + 2 * ML_VW]
    gi = p[..., ML_QKW + 2 * ML_VW:ML_QKW + 2 * ML_VW + ML_HEADS]
    gf = p[..., ML_QKW + 2 * ML_VW + ML_HEADS:]
    chunks = lambda t, dh: t.reshape(B, NC, CHUNK, ML_HEADS, dh).transpose(0, 3, 1, 2, 4).astype(jnp.float32)
    q = chunks(qk[..., :ML_QKW // 2], ML_QK) * (ML_QK ** -0.5)
    k = chunks(qk[..., ML_QKW // 2:], ML_QK)
    v = chunks(v, ML_V)
    gate_chunks = lambda t: t.reshape(B, NC, CHUNK, ML_HEADS).transpose(0, 3, 1, 2)
    log_i = gate_chunks(_softcap(gi.astype(jnp.float32) + b_i))
    log_f = gate_chunks(jax.nn.log_sigmoid(_softcap(gf.astype(jnp.float32) + b_f)))
    bcum = jnp.cumsum(log_f, -1)
    causal = jnp.tril(jnp.ones((CHUNK, CHUNK), dtype=bool))
    d_log = jnp.where(causal, bcum[..., :, None] - bcum[..., None, :] + log_i[..., None, :], NEG)
    m_intra = jnp.max(d_log, -1)
    g_tot = bcum[..., -1]
    loc = g_tot[..., None] - bcum + log_i
    m_loc = jnp.max(loc, -1)
    wl = jnp.exp(loc - m_loc[..., None])
    C_loc = jnp.einsum('bhcs,bhcsd,bhcse->bhcde', wl, k, v)
    n_loc = jnp.einsum('bhcs,bhcsd->bhcd', wl, k)
    init = (jnp.zeros((B, ML_HEADS, ML_QK, ML_V), jnp.float32),
            jnp.zeros((B, ML_HEADS, ML_QK), jnp.float32),
            jnp.zeros((B, ML_HEADS), jnp.float32))
    cm = lambda t: jnp.moveaxis(t, 2, 0)
    _, (C_prev, n_prev, m_prev) = lax.scan(_mlstm_chunk_step, init, (cm(g_tot), cm(m_loc), cm(C_loc), cm(n_loc)))
    C_prev, n_prev, m_prev = jnp.moveaxis(C_prev, 0, 2), jnp.moveaxis(n_prev, 0, 2), jnp.moveaxis(m_prev, 0, 2)
    inter = bcum + m_prev[..., None]
    m_t = jnp.maximum(inter, m_intra)
    w_inter = jnp.exp(inter - m_t)
    w_intra = jnp.exp(d_log - m_t[..., None]) * jnp.einsum('bhctd,bhcsd->bhcts', q, k)
    num = w_inter[..., None] * jnp.einsum('bhctd,bhcde->bhcte', q, C_prev) + jnp.einsum('bhcts,bhcse->bhcte', w_intra, v)
    den = w_inter * jnp.einsum('bhctd,bhcd->bhct', q, n_prev) + jnp.sum(w_intra, -1)
    den = jnp.maximum(jnp.abs(den), jnp.exp(-m_t))
    h = num / den[..., None]
    h = h * lax.rsqrt(jnp.mean(h * h, -1, keepdims=True) + EPS) * hn_w[:, None, None, :]
    h = h.transpose(0, 2, 3, 1, 4).reshape(B, S, ML_VW).astype(x.dtype)
    return (h * jax.nn.sigmoid(o)) @ w_out

def _swiglu(x, w_gu, w_down):
    gu = x @ w_gu
    return (jax.nn.silu(gu[..., :D_FF]) * gu[..., D_FF:]) @ w_down

def second_inputs(seed: int = 0) -> dict:
    key = jax.random.key(seed)
    ks = jax.random.split(key, 32)
    nrm = lambda i, shape, s: jax.random.normal(ks[i], shape, jnp.float32) * s
    D = D_MODEL
    lin = jnp.arange(D, dtype=jnp.float32) / (D - 1)
    return {
        "x": nrm(0, (BATCH, SEQ, D), 1.0),
        "c": nrm(1, (BATCH, D), 1.0),
        "ada_w": nrm(2, (DEPTH_2, D, 6 * D), 0.3 * D ** -0.5),
        "ada_b": nrm(3, (DEPTH_2, 6 * D), 0.02),
        "rw_mix": jax.random.uniform(ks[4], (N_RWKV, 6, D), jnp.float32),
        "rw_w_in": nrm(5, (N_RWKV, D, RW_IN), D ** -0.5),
        "rw_w0": jnp.broadcast_to(-6.0 + 5.0 * lin ** 1.5, (N_RWKV, D)) + nrm(6, (N_RWKV, D), 0.1),
        "rw_w2": nrm(7, (N_RWKV, LORA_W, D), 0.3 * LORA_W ** -0.5),
        "rw_a0": nrm(8, (N_RWKV, D), 0.1),
        "rw_a2": nrm(9, (N_RWKV, LORA_A, D), LORA_A ** -0.5),
        "rw_g2": nrm(10, (N_RWKV, LORA_G, D), LORA_G ** -0.5),
        "rw_k_k": 0.85 + nrm(11, (N_RWKV, D), 0.05),
        "rw_k_a": 1.0 + nrm(12, (N_RWKV, D), 0.05),
        "rw_r_k": nrm(13, (N_RWKV, RW_HEADS, RW_HEAD), 0.1),
        "rw_gn_w": 1.0 + nrm(14, (N_RWKV, D), 0.05),
        "rw_gn_b": nrm(15, (N_RWKV, D), 0.02),
        "rw_w_out": nrm(16, (N_RWKV, D, D), D ** -0.5),
        "ml_w_in": nrm(17, (N_MLSTM, D, ML_IN), D ** -0.5),
        "ml_conv_w": nrm(18, (N_MLSTM, CONV_W, ML_QKW), CONV_W ** -0.5),
        "ml_conv_b": nrm(19, (N_MLSTM, ML_QKW), 0.02),
        "ml_b_i": nrm(20, (N_MLSTM, ML_HEADS), 0.1),
        "ml_b_f": jnp.broadcast_to(jnp.linspace(3.0, 6.0, ML_HEADS, dtype=jnp.float32), (N_MLSTM, ML_HEADS)) + nrm(21, (N_MLSTM, ML_HEADS), 0.1),
        "ml_hn_w": 1.0 + nrm(22, (N_MLSTM, ML_HEADS, ML_V), 0.05),
        "ml_w_out": nrm(23, (N_MLSTM, D, D), D ** -0.5),
        "ffn_w_gu": nrm(24, (DEPTH_2, D, 2 * D_FF), D ** -0.5),
        "ffn_w_down": nrm(25, (DEPTH_2, D_FF, D), D_FF ** -0.5),
        "final_w": 1.0 + nrm(26, (D,), 0.05),
    }

def second_block(x, c, ada_w, ada_b, rw_mix, rw_w_in, rw_w0, rw_w2, rw_a0, rw_a2, rw_g2, rw_k_k, rw_k_a,
              rw_r_k, rw_gn_w, rw_gn_b, rw_w_out, ml_w_in, ml_conv_w, ml_conv_b, ml_b_i, ml_b_f, ml_hn_w,
              ml_w_out, ffn_w_gu, ffn_w_down, final_w):
    c_act = jax.nn.silu(c)
    for i in range(DEPTH_2):
        mod = c_act @ ada_w[i] + ada_b[i]
        sh1, sc1, g1, sh2, sc2, g2 = [t[:, None, :] for t in jnp.split(mod, 6, axis=-1)]
        h = _rms(x) * (1.0 + sc1) + sh1
        j = i // N_MIXERS
        if i % N_MIXERS == 0:
            y = _rwkv7_mix(h, rw_mix[j], rw_w_in[j], rw_w0[j], rw_w2[j], rw_a0[j], rw_a2[j], rw_g2[j],
                           rw_k_k[j], rw_k_a[j], rw_r_k[j], rw_gn_w[j], rw_gn_b[j], rw_w_out[j])
        else:
            y = _mlstm_mix(h, ml_w_in[j], ml_conv_w[j], ml_conv_b[j], ml_b_i[j], ml_b_f[j], ml_hn_w[j], ml_w_out[j])
        x = x + g1 * y
        h = _rms(x) * (1.0 + sc2) + sh2
        x = x + g2 * _swiglu(h, ffn_w_gu[i], ffn_w_down[i])
    return _rms(x) * final_w


def setup_inputs(seed=0):
    out = dict(first_inputs(seed))
    for name, value in second_inputs(seed + 1).items():
        if name != "x":
            out[name + "_2"] = value
    return out


def reference(
    x, c, positions, ada_w, ada_b, norm_mix_g, w_in, conv_w, ret_w_out, conv_w_out, mix_w_out,
    norm_ffn_g, ffn_w_gate, ffn_w_up, ffn_w_down, final_norm_g, c_2, ada_w_2, ada_b_2, rw_mix_2,
    rw_w_in_2, rw_w0_2, rw_w2_2, rw_a0_2, rw_a2_2, rw_g2_2, rw_k_k_2, rw_k_a_2, rw_r_k_2,
    rw_gn_w_2, rw_gn_b_2, rw_w_out_2, ml_w_in_2, ml_conv_w_2, ml_conv_b_2, ml_b_i_2, ml_b_f_2,
    ml_hn_w_2, ml_w_out_2, ffn_w_gu_2, ffn_w_down_2, final_w_2,
):
    x = first_block(
        x, c, positions, ada_w, ada_b, norm_mix_g, w_in, conv_w, ret_w_out, conv_w_out,
        mix_w_out, norm_ffn_g, ffn_w_gate, ffn_w_up, ffn_w_down, final_norm_g,
    )
    return second_block(
        x, c_2, ada_w_2, ada_b_2, rw_mix_2, rw_w_in_2, rw_w0_2, rw_w2_2, rw_a0_2, rw_a2_2,
        rw_g2_2, rw_k_k_2, rw_k_a_2, rw_r_k_2, rw_gn_w_2, rw_gn_b_2, rw_w_out_2, ml_w_in_2,
        ml_conv_w_2, ml_conv_b_2, ml_b_i_2, ml_b_f_2, ml_hn_w_2, ml_w_out_2, ffn_w_gu_2,
        ffn_w_down_2, final_w_2,
    )


_drawn_inputs = setup_inputs


def setup_inputs(seed=0):
    import zlib

    import numpy as np

    out = dict(_drawn_inputs(seed))
    spreads = {}
    factors = {'ada_b': 3.178,
     'norm_mix_g': 8.0,
     'norm_ffn_g': 64.0,
     'final_norm_g': 2.8,
     'rw_w2_2': 8.0,
     'rw_a0_2': 8.0,
     'rw_k_k_2': 46.748,
     'rw_k_a_2': 23.237,
     'rw_gn_w_2': 31.853,
     'rw_gn_b_2': 64.0,
     'ml_conv_b_2': 8.0,
     'ml_b_i_2': 64.0,
     'ml_hn_w_2': 35.489,
     'ret_w_out': 4.312}
    for name, (base, spread) in spreads.items():
        noise = np.random.default_rng([zlib.crc32(name.encode()), seed]).standard_normal(out[name].shape)
        drawn = base * np.exp(spread * noise) if base else spread * noise
        out[name] = __import__('jax').numpy.asarray(drawn.astype(out[name].dtype))
    for name, factor in factors.items():
        out[name] = (out[name] * factor).astype(out[name].dtype)
    return out
```

```python
from contextlib import ExitStack

import concourse.bass as bass
import numpy as np
from concourse import mybir

F32 = mybir.dt.float32
F32R = mybir.dt.float32r
I32 = mybir.dt.int32
ALU = mybir.AluOpType
ACT = mybir.ActivationFunctionType

P = 128
D = 1024
T = 256
NF = D // P
PLANE = NF * T
FFN = 2816
NH = FFN // P
EPS = 1e-6
GN_EPS = 64e-5
KAPPA = float(np.exp(-0.5))
CH = 64
LEVELS = 5
CAP = 15.0

RING = 4
KT = 4
COLS = 512
SLOT = KT * COLS
NPLANES = 15

C_ID, C_ONE, C_BLK, C_MASK, C_LVL = 0, 128, 256, 384, 640
C_CAUS = C_LVL + 128 * (LEVELS + 1)
C_FREQ = C_CAUS + P
C_ZERO = C_FREQ + 2
NCONST = C_ZERO + 64
N_CONST_DMAS = 2
TWO_PI = (6.28125, 0.0019350051879882812, 3.019916050561733e-07)

VECS = [("c", 8), ("c_2", 8), ("ada_b", 48), ("ada_b_2", 96), ("norm_mix_g", 8), ("norm_ffn_g", 8),
        ("final_norm_g", 8), ("conv_w", 24), ("rw_mix_2", 48), ("rw_w0_2", 8), ("rw_a0_2", 8), ("rw_k_k_2", 8),
        ("rw_k_a_2", 8), ("rw_r_k_2", 8), ("rw_gn_w_2", 8), ("rw_gn_b_2", 8), ("ml_conv_w_2", 32),
        ("ml_conv_b_2", 8), ("ml_hn_w_2", 8), ("final_w_2", 8)]
VOFF = {}
_n = 0
for _name, _w in VECS:
    VOFF[_name] = _n
    _n += _w
NVEC = _n


def shape_constants():
    c = np.zeros((P, NCONST), np.float32)
    i = np.arange(P)
    s, t = i[:, None], i[None, :]
    c[:, C_ID:C_ID + P] = s == t
    c[:, C_ONE:C_ONE + P] = 1.0
    c[:, C_BLK:C_BLK + P] = s // 64 == t // 64
    same = s // CH == t // CH
    strict, incl = same & (s < t), same & (s <= t)
    c[:, C_MASK:C_MASK + 256] = np.concatenate([strict, incl], 1)
    for lv in range(LEVELS + 1):
        half = 1 << lv
        off = (s // (2 * half) == t // (2 * half)) & (s % (2 * half) < half) & (t % (2 * half) >= half)
        c[:, C_LVL + lv * P:C_LVL + (lv + 1) * P] = off
    c[:, C_CAUS:C_CAUS + P] = s <= t
    c[:, C_FREQ] = 1.0 / (np.float32(10000.0) ** (np.arange(0, P, 2, dtype=np.float32) / np.float32(P)))[i % 64]
    c[:, C_FREQ + 1] = np.where(i < 64, 1.0, -1.0)
    h = np.arange(NF, dtype=np.float32)
    lg = np.log(1.0 - 2.0 ** (-5.0 - h.astype(np.float64)))
    rel = np.arange(T)[None, :] - s
    dec = np.where(rel[:, None, :] >= 0, np.exp(lg[None, :, None] * np.maximum(rel, 0)[:, None, :]), 0.0) * P ** -0.5
    dec = np.concatenate([dec, dec[:, :, 0:P]], 2).astype(np.float32).reshape(P, NF * 384)
    sel = np.zeros((NF, NF, P), np.float32)
    for k in range(NF):
        sel[k, k, :] = 1.0
    return c, dec, sel.reshape(NF, NF * P)


def build(nc, d):
    ctx = ExitStack()
    with ctx:
        def sb(name, shape, dt=F32):
            return ctx.enter_context(nc.sbuf_tensor(name, shape, dt))

        sems = {}

        def S(name):
            if name not in sems:
                sems[name] = ctx.enter_context(nc.semaphore(name))
            return sems[name]

        ring = sb("ring", [P, RING, SLOT])
        whi = sb("whi", [P, 2, SLOT], F32R)
        wlo = sb("wlo", [P, 2, SLOT], F32R)
        X = sb("X", [P, NF, T])
        cst = sb("cst", [P, NCONST])
        vec = sb("vec", [P, NVEC])
        mods = sb("mods", [P, 3, 48])
        silu_c = sb("silu_c", [P, 16])
        nscale = sb("nscale", [P, NF])
        gateb = sb("gateb", [NF, 2])
        adaacc = sb("adaacc", [P, COLS])
        rs = sb("rs", [P, T])
        state = sb("state", [P, NF, P])
        pend = sb("pend", [P, NF, 4])
        parts_r = {}
        for first, n in ((0, 1), (1, 1), (2, 1), (3, 1), (4, 1), (5, 1), (2, 3), (5, 3)):
            with ExitStack() as at_plane:
                if first:
                    at_plane.enter_context(nc.sbuf_tensor(f"below{first}_{n}", [P, first, PLANE], F32))
                parts_r[first, n] = at_plane.enter_context(nc.sbuf_tensor(f"parts{first}_{n}", [P, n, PLANE], F32R))
        arena = sb("arena", [P, NPLANES, PLANE])

        acc = [ctx.enter_context(nc.psum_tensor(f"acc{b}", [P, 1024], F32)) for b in range(2)]
        aux = [ctx.enter_context(nc.psum_tensor(f"aux{b}", [P, 512], F32)) for b in range(4)]

        def pl(i):
            return arena[:, i, :].rearrange("p (f t) -> p f t", t=T)

        def plr(i):
            return parts_r[i, 1][:, 0, :].rearrange("p (f t) -> p f t", t=T)

        def bcast(ap, n):
            return ap.rearrange("p (a t) -> p a t", a=1).to_broadcast([ap.shape[0], n, ap.shape[1]])

        def cc(o, n=P):
            return cst[:, o:o + n]

        def V(name, i=0, n=1, rows=P):
            return vec[0:rows, VOFF[name] + i:VOFF[name] + i + n]

        ident, ones, blk = cc(C_ID), cc(C_ONE), cc(C_BLK)

        block = ctx.enter_context(nc.Block())

        acc_jobs, aux_jobs = {}, {}

        def wait_filled(e, kind, name):
            a, n = (acc_jobs, 2) if kind == "acc" else (aux_jobs, 4)
            a = a[name]
            e.wait_ge(S(f"{kind}_filled{a % n}"), a // n + 1)
            return (acc if kind == "acc" else aux)[a % n]

        def drained(kind, name):
            a, n = (acc_jobs, 2) if kind == "acc" else (aux_jobs, 4)
            return S(f"{kind}_drained{a[name] % n}")

        def wait_drained(e, kind, name):
            a, n = (acc_jobs, 2) if kind == "acc" else (aux_jobs, 4)
            a = a[name]
            e.wait_ge(S(f"{kind}_drained{a % n}"), a // n + 1)


        slots = []
        freed = {}
        split_of, used = [], []
        ada_slots = []
        job_last = {}
        after_job = {}

        def add_slot(kind, dst, srcs):
            slots.append((kind, dst, srcs))
            return len(slots) - 1

        def landed(e, j):
            n = sum(len(slots[i][2]) for i in range(j % RING, j + 1, RING))
            e.wait_ge(S(f"w_landed{j % RING}"), 16 * n)

        def rows_of(w, k0, n, c0, ncols):
            return (P, 0, n, ncols, w[k0 * P:(k0 + n) * P, c0:c0 + ncols].rearrange("(k p) n -> p k n", p=P))

        def ada_group():
            g = len(ada_slots)
            if g < 36:
                w = (d["ada_w"][0], d["ada_w_2"][0], d["ada_w_2"][1])[g // 12]
                ada_slots.append([add_slot("ada", None, [rows_of(w, KT * j, KT, (g % 12) * COLS, COLS)])
                                  for j in range(2)])

        A_IN, B_IN = (0, 1), (2, 3)
        HID_HI, HID_LO = 2, 5
        AR = arena[:, 4:6, :].rearrange("p a n -> p (a n)").rearrange("p (f g r t) -> p f g r t", f=NF, g=2, r=2)
        MM = arena[:, 11:15, :].rearrange("p a n -> p (a n)").rearrange("p (h q) -> p h q", q=512)
        TI = arena[:, 2, :].rearrange("p (h t) -> p h t", t=P)
        TT = arena[:, 3, :].rearrange("p (h t) -> p h t", t=P)
        NM = arena[:, 6, 0:1024].rearrange("p (b n) -> p b n", n=512)
        UU = arena[:, 6, 1024:2048].rearrange("p (b n) -> p b n", n=512)
        BTOK, KTOK = arena[:, 9, 0:1024], arena[:, 9, 1024:2048]
        XSA = arena[:, 2, 0:1024]
        SAT = arena[:, 2, 1024:2048]
        dec = arena[:, 11:13, :].rearrange("p a n -> p (a n)")[:, 0:NF * 384].rearrange("p (h t) -> p h t", t=384)
        cosb, sinb = arena[:, 12, 1024:1280], arena[:, 12, 1280:1536]
        posi = arena[:, 12, 1536:1792].bitcast(I32)
        pbuf = arena[:, 4, 0:768].rearrange("p (b t) -> p b t", t=384)
        lora = arena[:, 12, 0:1024].rearrange("p (b t) -> p b t", t=T)
        selm = arena[0:NF, 7, 0:1024].rearrange("p (h t) -> p h t", t=P)
        ucol = arena[:, 7, 1024:1040]
        gts = arena[0:NF, 8, 0:2048].rearrange("p (b t) -> p b t", t=T)
        dbuf = arena[:, 9, 0:1920].rearrange("p (b t) -> p b t", t=384)
        ebuf = arena[:, 10, 0:1024].rearrange("p (b t) -> p b t", t=T)
        silug = arena[:, 8, :].rearrange("p (b m t) -> p b m t", b=2, t=T)
        prod = arena[:, 9, :].rearrange("p (b m t) -> p b m t", b=2, t=T)

        def hid(base):
            return parts_r[base, 3][:, :, :].rearrange("p a n -> p (a n)")[:, 0:NH * T].rearrange(
                "p (f t) -> p f t", t=T)

        def tok(plane):
            return arena[:, plane, :].rearrange("p (g n) -> p g n", g=2)

        FW = [512] * 5 + [256]

        @block.tensor
        def _(pe):
            n_used, n_in = [0], [0]

            def begin(kind, name):
                jobs, n = (acc_jobs, 2) if kind == "acc" else (aux_jobs, 4)
                a = jobs[name] = len(jobs)
                if a >= n:
                    pe.wait_ge(S(f"{kind}_drained{a % n}"), a // n)
                return (acc if kind == "acc" else aux)[a % n], S(f"{kind}_filled{a % n}"), a // n + 1

            def mm(out, lhsT, rhs, start, stop):
                return pe.matmul(out, lhsT, rhs, start=start, stop=stop, skip_group_check=True)

            def ada_reduce(g):
                ps, filled, _ = begin("aux", f"ada{g}")
                pe.wait_ge(S("ada_summed"), g + 1)
                for m in range(4):
                    last = mm(ps[:, m:m + 1], adaacc[:, m * P:(m + 1) * P], ones[:, 0:1], m == 0, True)
                last.then_inc(filled, 1)

            def new_input(n=NF):
                base = n_in[0]
                n_in[0] += n
                return lambda k: pe.wait_ge(S("in_ready"), base + k + 1)

            streamed = []

            def stream(name, w, c0, ncols, nk, x_hi, x_lo, ready=None, tiles=None, srcs=None, reuse=None):
                tiles = tiles or [(m * P, P, m) for m in range(ncols // P)]
                todo = []
                if reuse is not None:
                    todo = [(0, nk, reuse)]
                else:
                    for k0 in range(0, nk, KT if ncols > 256 else 8):
                        n = min(KT if ncols > 256 else 8, nk - k0)
                        src = srcs if srcs else [rows_of(w, k0, n, c0, ncols)]
                        todo.append((k0, n, add_slot("split" if x_lo is not None else "raw", None, src)))
                ps, filled, nth = begin("acc", name)
                for k0, n, j in todo:
                    if x_lo is not None:
                        q = len(split_of)
                        split_of.append(j)
                        pe.wait_ge(S("w_split"), q + 1)
                        parts = [(whi[:, q % 2, :], x_hi), (wlo[:, q % 2, :], x_hi), (whi[:, q % 2, :], x_lo)]
                    else:
                        landed(pe, j)
                        parts = [(ring[:, j % RING, :], x_hi)]
                    for i_m, (off, wd, m) in enumerate(tiles):
                        for k in range(n):
                            if ready and i_m == 0:
                                ready(k0 + k)
                            rows = P if not srcs or k < len(srcs) - 1 else srcs[-1][0]
                            for i, (wt, x) in enumerate(parts):
                                o = k * ncols + off
                                last = mm(ps[0:wd, m * T:(m + 1) * T], wt[0:rows, o:o + wd],
                                          x[0:rows, k0 + k, :], k0 + k == 0 and i == 0 and m % 2 == 0,
                                          k0 + k == nk - 1 and i == len(parts) - 1)
                    if k0 + n < nk:
                        n_used[0] += 1
                        last.then_inc(S("w_used"), 1)
                        end = (S("w_used"), n_used[0])
                    else:
                        last.then_inc(filled, 1)
                        end = (filled, nth)
                    if x_lo is not None:
                        used.append(end)
                    else:
                        freed[j] = end
                job_last[name] = max(j for _, _, j in todo)
                after_job[name] = []
                while len(streamed) < len(ada_slots) and ada_slots[len(streamed)][1] < job_last[name]:
                    g = len(streamed)
                    streamed.append(g)
                    ada_reduce(g)
                    after_job[name].append(g)
                n_jobs[0] += 1
                if n_jobs[0] % 2 == 0 and reuse is None:
                    ada_group()
                return todo[-1][2]

            n_jobs = [0]

            def norm(i):
                ps, filled, _ = begin("aux", f"norm{i}")
                for f in range(NF):
                    pe.wait_ge(S("sq_ready"), NF * i + f + 1)
                    last = mm(ps[:, 0:T], ones, pl(14)[:, f, :], f == 0, f == NF - 1)
                last.then_inc(filled, 1)

            def sums(name, sem, lhsT, plane, j):
                ps, filled, _ = begin("aux", f"{name}{j}")
                pe.wait_ge(S(sem), j + 1)
                mm(ps[:, :], lhsT, arena[:, plane, 512 * j:512 * (j + 1)], True, True).then_inc(filled, 1)

            def to_tokens(name, plane, g, b, waits):
                ps, filled, _ = begin("aux", f"{name}{g}{b}")
                waits()
                for m in range(4):
                    last = pe.matmul(ps[:, m * P:(m + 1) * P], pl(plane)[:, 4 * b + m, g * P:(g + 1) * P], ident,
                                     is_transpose=True, start=m == 0, stop=True, skip_group_check=True)
                last.then_inc(filled, 1)

            def ffn(l, wg, cg, wu, cu, wd):
                x = (plr(0), plr(1))
                r = new_input()
                for c, n in enumerate(FW):
                    stream(f"fg{l}{c}", wg, cg + COLS * c, n, NF, *x, ready=r if c == 0 else None)
                    stream(f"fu{l}{c}", wu, cu + COLS * c, n, NF, *x)
                r = new_input(NH)
                for c in range(2):
                    stream(f"fd{l}{c}", wd, COLS * c, COLS, NH, hid(HID_HI), hid(HID_LO), ready=r if c == 0 else None)

            def pair(name, w, c0, planes, ready=None):
                for c in range(2):
                    stream(f"{name}{c}", w, c0 + COLS * c, COLS, NF, plr(planes[0]), plr(planes[1]),
                           ready=ready if c == 0 else None)

            for g in range(4):
                ada_group()
            pe.wait_ge(S("consts"), 16 * N_CONST_DMAS)
            norm(0)
            for g in range(4):
                streamed.append(g)
                ada_reduce(g)
            r = new_input()
            w_in = d["w_in"][0]
            pair("q", w_in, 0, A_IN, r)
            pair("k", w_in, D, A_IN)
            pair("v", w_in, 2 * D, A_IN)
            pair("g", w_in, 3 * D, A_IN)
            for g in range(2):
                for b in range(2):
                    to_tokens("vt", 4, g, b, lambda: wait_drained(pe, "acc", f"v{b}"))
            pair("b", w_in, 4 * D, A_IN)

            def ret_scores(h):
                ps, filled, _ = begin("aux", f"rs{h}")
                pe.wait_ge(S("roped"), 2)
                mm(ps[:, 0:T], pl(3)[:, h, 0:P], pl(2)[:, h, :], True, True)
                mm(ps[:, T:T + P], pl(3)[:, h, P:T], pl(2)[:, h, P:T], False, True).then_inc(filled, 1)

            def weighted(name, h, w, vplane, sem, n, den):
                ps, filled, _ = begin("aux", f"{name}{h}")
                pe.wait_ge(S(sem), n)
                last = mm(ps[:, 0:T], tok(vplane)[:, 0, h * P:(h + 1) * P], w[:, 0:T], True, False)
                last = mm(ps[:, P:T], tok(vplane)[:, 1, h * P:(h + 1) * P], w[:, T:T + P], False, True)
                if den:
                    last = mm(ps[:, T:2 * T], ones, w[:, 0:T], False, False)
                    last = mm(ps[:, T + P:2 * T], ones, w[:, T:T + P], False, True)
                last.then_inc(filled, 1)

            def ret_y(h):
                if h == 0:
                    for g in range(2):
                        for b in range(2):
                            wait_drained(pe, "aux", f"vt{g}{b}")
                weighted("ry", h, pbuf[:, h % 2, :], 5, "ret_w", h + 1, False)

            ret_scores(0)
            ret_scores(1)
            for n, (c0, nm) in enumerate([(5, "c"), (6, "u")]):
                for c in range(2):
                    stream(f"{nm}{c}", w_in, c0 * D + COLS * c, COLS, NF, plr(0), plr(1))
                    h = 2 * (2 * n + c)
                    ret_y(h)
                    ret_y(h + 1)
                    if h + 2 < NF:
                        ret_scores(h + 2)
                        ret_scores(h + 3)
            stream("ga0", w_in, 7 * D, COLS, NF, plr(0), plr(1))
            for h in range(NF):
                wait_drained(pe, "aux", f"ry{h}")
            for j in range(4):
                sums("rmean", "ry_all", ones, 13, j)
            stream("ga1", w_in, 7 * D + COLS, COLS, NF, plr(0), plr(1))
            for j in range(4):
                sums("rvar", "ret_sq", ones, 14, j)
            pair("gb", w_in, 8 * D, A_IN)
            pair("co", d["conv_w_out"][0], 0, B_IN, new_input())
            pair("ro", d["ret_w_out"][0], 0, A_IN, new_input())
            pair("mo", d["mix_w_out"][0], 0, B_IN, new_input())
            norm(1)
            ffn(0, d["ffn_w_gate"][0], 0, d["ffn_w_up"][0], 0, d["ffn_w_down"][0])
            norm(2)

            norm(3)
            w_in = d["rw_w_in_2"][0]

            def small(name, w, c0, ncols, x, ready, tiles):
                stream(name, w, c0, ncols, NF, x, None, ready=ready, tiles=tiles)

            small("wl", w_in, D, 64, pl(0), new_input(), [(0, 64, 0)])
            small("al", w_in, 3 * D + 64, 64, pl(1), new_input(), [(0, 64, 0)])
            small("gl", w_in, 3 * D + 128, 160, pl(4), new_input(), [(0, P, 0), (P, 32, 1)])
            four = lambda c: [(c * COLS + m * P, P, m) for m in range(4)]
            for nm, src, w, x in (("w2", "wl", d["rw_w2_2"][0], lora[:, 0:1, :]),
                                  ("a2", "al", d["rw_a2_2"][0], lora[:, 1:2, :]),
                                  ("g2", "gl", d["rw_g2_2"][0], lora[:, 2:4, :])):
                wait_drained(pe, "acc", src)
                if nm == "g2":
                    srcs = [(P, 0, 1, D, w[0:P, :].rearrange("(k p) n -> p k n", k=1)),
                            (32, D, 1, D, w[P:P + 32, :].rearrange("(k p) n -> p k n", k=1))]
                    nk = 2
                else:
                    srcs = [(64, 0, 1, D, w.rearrange("(k p) n -> p k n", k=1))]
                    nk = 1
                j = stream(nm + "0", w, 0, D, nk, x, None, tiles=four(0), srcs=srcs)
                stream(nm + "1", w, 0, D, nk, x, None, tiles=four(1), srcs=srcs, reuse=j)
            pair("r", w_in, 0, (0, 1), new_input())
            pair("kk", w_in, D + 64, (4, 5), new_input())
            pair("vv", w_in, 2 * D + 64, (0, 1), new_input())
            for j in range(4):
                sums("kkn", "kk_sq", blk, 3, j)
            for j in range(4):
                sums("bon", "rk_ready", blk, 13, j)
            for g in range(2):
                for b in range(2):
                    to_tokens("wt", 11, g, b, lambda: wait_drained(pe, "acc", f"vv{b}"))
            rows = [slice(0, 64), slice(64, 128)]
            bh, kh = pl(7), pl(10)
            for g in range(2):
                gs = slice(g * P, (g + 1) * P)
                for h in range(16):
                    f, i = h // 2, h % 2
                    ps, filled, _ = begin("aux", f"m{g}{h}")
                    if h == 0 and g == 0:
                        pe.wait_ge(S("hats"), 6)
                    mm(ps[:, 0:T], bh[rows[i], f, gs], AR[rows[i], f, g, :, :], True, True)
                    mm(ps[:, T:2 * T], kh[rows[i], f, gs], AR[rows[i], f, g, :, :], False, True).then_inc(filled, 1)
                for b in range(4):
                    ps, filled, _ = begin("aux", f"t{g}{b}")
                    pe.wait_ge(S("tt_ready"), (LEVELS + 1) * 4 * g + b + 1)
                    for m in range(4):
                        last = pe.matmul(ps[:, m * P:(m + 1) * P], TT[:, 4 * b + m, :], ident, is_transpose=True,
                                         start=m == 0, stop=True, skip_group_check=True)
                    last.then_inc(filled, 1)
                for nm, src in (("bt", 7), ("kt", 10)):
                    for b in range(2):
                        to_tokens(nm, src, g, b, lambda: None)
                for lv in range(1, LEVELS + 1):
                    for b in range(4):
                        ps, filled, _ = begin("aux", f"u{g}{lv}{b}")
                        n = (LEVELS * g + lv - 1) * 4 + b
                        pe.wait_ge(S("nm_ready"), n + 1)
                        wait_drained(pe, "aux", f"t{g}{b}" if lv == 1 else f"t{g}{lv - 1}{b}")
                        for m in range(4):
                            last = mm(ps[:, m * P:(m + 1) * P], NM[:, n % 2, m * P:(m + 1) * P], TI[:, 4 * b + m, :],
                                      m == 0, True)
                        last.then_inc(filled, 1)
                        ps, filled, _ = begin("aux", f"v{g}{lv}{b}")
                        wait_drained(pe, "aux", f"u{g}{lv}{b}")
                        for m in range(4):
                            last = mm(ps[:, m * P:(m + 1) * P], UU[:, n % 2, m * P:(m + 1) * P], TT[:, 4 * b + m, :],
                                      m == 0, True)
                        last.then_inc(filled, 1)
                    if lv < LEVELS:
                        for b in range(4):
                            ps, filled, _ = begin("aux", f"t{g}{lv}{b}")
                            wait_drained(pe, "aux", f"v{g}{lv}{b}")
                            for m in range(4):
                                last = pe.matmul(ps[:, m * P:(m + 1) * P], TT[:, 4 * b + m, :], ident,
                                                 is_transpose=True, start=m == 0, stop=True, skip_group_check=True)
                            last.then_inc(filled, 1)
                yps, yfilled, _ = begin("acc", f"y{g}")
                for c in range(2):
                    cs = slice(64 * c, 64 * c + 64)
                    n = 2 * g + c
                    pe.wait_ge(S("state_ready"), 4 * n + 1)
                    for f in range(NF):
                        mm(yps[:, f * P + 64 * c:f * P + 64 * c + 64], state[:, f, :], AR[:, f, g, 1, cs],
                           f % 4 == 0 and c == 0, False)
                    for b in range(2):
                        ps, filled, _ = begin("aux", f"x{n}{b}")
                        if b == 0 and c == 0:
                            for bb in range(4):
                                wait_drained(pe, "aux", f"v{g}{LEVELS}{bb}")
                            for bb in range(2):
                                wait_drained(pe, "aux", f"wt{g}{bb}")
                        for m in range(4):
                            f = 4 * b + m
                            mm(ps[cs, m * P:(m + 1) * P], AR[:, f, g, 0, cs], state[:, f, :], m == 0, False)
                            for i in range(2):
                                o = m * P + 64 * i
                                last = mm(ps[cs, o:o + 64], MM[:, 2 * f + i, T + 64 * c:T + 64 * c + 64],
                                          tok(0)[:, g, f * P + 64 * i:f * P + 64 * i + 64], False, True)
                        last.then_inc(filled, 1)
                    for b in range(2):
                        ps, filled, _ = begin("aux", f"sa{n}{b}")
                        wait_drained(pe, "aux", f"x{n}{b}")
                        for m in range(8):
                            h = 8 * b + m
                            last = mm(ps[cs, 64 * m:64 * m + 64], TT[cs, h, cs], XSA[cs, 64 * h:64 * h + 64],
                                      m == 0, True)
                        last.then_inc(filled, 1)
                    for b in range(2):
                        ps, filled, _ = begin("aux", f"st{n}{b}")
                        wait_drained(pe, "aux", f"sa{n}{b}")
                        if b == 0 and c == 0:
                            for bb in range(2):
                                wait_drained(pe, "aux", f"bt{g}{bb}")
                                wait_drained(pe, "aux", f"kt{g}{bb}")
                        for m in range(4):
                            f = 4 * b + m
                            fs = slice(f * P, (f + 1) * P)
                            mm(ps[:, m * P:(m + 1) * P], BTOK[cs, fs], SAT[cs, fs], m == 0, False)
                            last = mm(ps[:, m * P:(m + 1) * P], KTOK[cs, fs], tok(0)[cs, g, fs], False, True)
                        last.then_inc(filled, 1)
                for h in range(16):
                    f, i = h // 2, h % 2
                    o = yps[rows[i], f * P:(f + 1) * P]
                    mm(o, SAT[:, 64 * h:64 * h + 64], MM[:, h, P:2 * P], False, False)
                    last = mm(o, tok(0)[:, g, 64 * h:64 * h + 64], MM[:, h, 3 * P:4 * P], False, True)
                last.then_inc(yfilled, 1)
            wait_drained(pe, "acc", "y1")
            for j in range(4):
                sums("wmean", "wy_all", blk, 7, j)
            for j in range(4):
                sums("wvar", "rw_sq", blk, 6, j)
            pair("wo", d["rw_w_out_2"][0], 0, (4, 5), new_input())
            norm(4)
            gu = d["ffn_w_gu_2"]
            ffn(1, gu[0], 0, gu[0], FFN, d["ffn_w_down_2"][0])

            norm(5)
            w_in = d["ml_w_in_2"][0]
            r = new_input()
            stream("gt", w_in, 3 * D, 16, NF, pl(13), None, ready=r, tiles=[(0, NF, 0), (NF, NF, 1)])
            pair("qk", w_in, 0, A_IN)
            pair("mv", w_in, D, A_IN)
            pair("o", w_in, 2 * D, A_IN)
            ps, filled, _ = begin("aux", "ut")
            pe.wait_ge(S("gates"), 2)
            for g in range(2):
                last = pe.matmul(ps[:, NF * g:NF * (g + 1)], gts[:, 3, g * P:(g + 1) * P], cst[0:NF, C_ID:C_ID + NF],
                                 is_transpose=True, start=g == 0, stop=True, skip_group_check=True)
            last.then_inc(filled, 1)
            for g in range(2):
                for b in range(2):
                    to_tokens("mt", 4, g, b, lambda: wait_drained(pe, "acc", f"mv{b}"))

            def ml_num(h):
                if h == 0:
                    for g in range(2):
                        for b in range(2):
                            wait_drained(pe, "aux", f"mt{g}{b}")
                weighted("nd", h, dbuf[:, 3 + h % 2, :], 6, "ml_w", h + 1, True)

            for h in range(NF):
                ps, filled, _ = begin("aux", f"gb{h}")
                mm(ps[:, :], selm[:, h, :], gts[:, 4:6, :].rearrange("p a t -> p (a t)"), True, True)\
                    .then_inc(filled, 1)
                ps, filled, _ = begin("aux", f"ms{h}")
                pe.wait_ge(S("ml_act"), NF)
                rr = rows[h % 2]
                q, k = pl(3)[rr, h // 2, :], pl(3)[rr, 4 + h // 2, :]
                mm(ps[:, 0:T], k[:, 0:P], q, True, True)
                mm(ps[:, T:T + P], k[:, P:T], q[:, P:T], False, True).then_inc(filled, 1)
                if h >= 1:
                    ml_num(h - 1)
            ml_num(NF - 1)
            for j in range(4):
                sums("msq", "ml_sq", ones, 12, j)
            pair("lo", d["ml_w_out_2"][0], 0, A_IN, new_input())
            norm(6)
            ffn(2, gu[1], 0, gu[1], FFN, d["ffn_w_down_2"][1])
            norm(7)

        @block.scalar
        def _(act):
            count = {}

            def do(ins, sig="act_step"):
                count[sig] = count.get(sig, 0) + 1
                last[0] = sig
                ins.then_inc(S(sig), 1)

            last = [None]

            def fence(sig=None):
                act.wait_ge(S(sig or last[0]), count[sig or last[0]])

            f_ = act.activation
            split_at = [0]

            def pump(upto):
                while split_at[0] < len(split_of) and split_of[split_at[0]] <= upto:
                    q = split_at[0]
                    j = split_of[q]
                    _, _, srcs = slots[j]
                    n = sum(s[2] * s[3] for s in srcs)
                    landed(act, j)
                    if q >= 2:
                        act.wait_ge(*used[q - 2])
                    f_(whi[:, q % 2, 0:n], ring[:, j % RING, 0:n], ACT.Copy).then_inc(S("w_hi"), 1)
                    split_at[0] += 1

            def job(name):
                pump(job_last[name] + 1)

            def drain(kind, name, out, in_, func, last=True, **kw):
                ins = f_(out, in_, func, **kw)
                if last:
                    ins.then_inc(drained(kind, name), 1)
                else:
                    do(ins)

            def drain4(name, plane, c, func):
                job(name)
                ps = wait_filled(act, "acc", name)
                drain("acc", name, arena[:, plane, 1024 * c:1024 * (c + 1)], ps[:, :], func)

            def norm(i):
                for f in range(NF):
                    if i == 0:
                        if f == 0:
                            act.wait_ge(S("x_in"), 16)
                    else:
                        act.wait_ge(S("x_ready"), NF * (i - 1) + f + 1)
                    do(f_(pl(14)[:, f, :], X[:, f, :], ACT.Square), "sq_ready")
                ps = wait_filled(act, "aux", f"norm{i}")
                drain("aux", f"norm{i}", rs[:, :], ps[:, 0:T], ACT.Sqrt, scale=1.0 / D, bias=EPS)

            def head_sqrt(name, plane, scale, eps, j):
                ps = wait_filled(act, "aux", f"{name}{j}")
                drain("aux", f"{name}{j}", arena[:, plane, 512 * j:512 * (j + 1)], ps[:, :], ACT.Sqrt,
                      scale=scale, bias=eps)

            def ffn(l):
                for c, n in enumerate(FW):
                    job(f"fg{l}{c}")
                    ps = wait_filled(act, "acc", f"fg{l}{c}")
                    if c >= 2:
                        act.wait_ge(S("prod_ready"), len(FW) * l + c - 1)
                    drain("acc", f"fg{l}{c}", silug[:, c % 2, 0:n // P, :].rearrange("p m t -> p (m t)"),
                          ps[:, 0:2 * n], ACT.Silu)
                    job(f"fu{l}{c}")
                for c in range(2):
                    job(f"fd{l}{c}")

            act.dma_start(X[:, :, :], d["x"]).then_inc(S("x_in"), 16)
            act.dma_start(cst[:, :], d["cst"]).then_inc(S("consts"), 16)
            act.dma_start(vec[:, :], d["vec"]).then_inc(S("consts"), 16)
            act.dma_start(posi, d["positions"].partition_broadcast(P)).then_inc(S("tables"), 16)
            act.dma_start(arena[:, 11:13, :].rearrange("p a n -> p (a n)")[:, 0:NF * 384], d["dec"])\
                .then_inc(S("tables"), 16)
            act.wait_ge(S("consts"), 32)
            do(f_(silu_c[:, :], vec[:, 0:16], ACT.Silu), "c_ready")
            norm(0)
            act.wait_ge(S("angles"), 2)
            do(f_(sinb, pl(14)[:, 2, :], ACT.Sin), "trig")
            do(f_(cosb, pl(14)[:, 3, :], ACT.Sin), "trig")
            for nm, plane, func in (("q", 2, ACT.Copy), ("k", 3, ACT.Copy), ("v", 4, ACT.Copy), ("g", 6, ACT.Silu),
                                    ("b", 7, ACT.Copy)):
                for c in range(2):
                    drain4(f"{nm}{c}", plane, c, func)
            def tokens(name, g, b, dst):
                ps = wait_filled(act, "aux", f"{name}{g}{b}")
                drain("aux", f"{name}{g}{b}", dst[:, 512 * b:512 * (b + 1)], ps[:, :], ACT.Copy)

            def ret_drain(h):
                ps = wait_filled(act, "aux", f"ry{h}")
                drain("aux", f"ry{h}", pl(13)[:, h, :], ps[:, 0:T], ACT.Copy)

            for n in range(4):
                if n < 2:
                    drain4(f"c{n}", 8, n, ACT.Copy)
                else:
                    job(f"u{n - 2}")
                ret_drain(2 * n)
                ret_drain(2 * n + 1)
            do(act.nop(), "ry_all") if False else None
            drain4("ga0", 9, 0, ACT.Sigmoid)
            for j in range(4):
                act.wait_ge(S("ret_c"), j + 1)
                do(f_(arena[:, 14, 512 * j:512 * (j + 1)], arena[:, 13, 512 * j:512 * (j + 1)], ACT.Square), "ret_sq")
            drain4("ga1", 9, 1, ACT.Sigmoid)
            for j in range(4):
                head_sqrt("rvar", 14, 1.0 / P, EPS, j)
            drain4("gb0", 10, 0, ACT.Sigmoid)
            drain4("gb1", 10, 1, ACT.Sigmoid)
            for nm in ("co", "ro", "mo"):
                for c in range(2):
                    job(f"{nm}{c}")
            norm(1)
            ffn(0)
            norm(2)
            norm(3)

            for nm, rws, b, func in (("wl", 64, 0, ACT.Tanh), ("al", 64, 1, ACT.Copy)):
                job(nm)
                ps = wait_filled(act, "acc", nm)
                drain("acc", nm, lora[0:rws, b, :], ps[0:rws, 0:T], func)
            job("gl")
            ps = wait_filled(act, "acc", "gl")
            do(f_(lora[:, 2, :], ps[:, 0:T], ACT.Sigmoid))
            drain("acc", "gl", lora[0:32, 3, :], ps[0:32, T:2 * T], ACT.Sigmoid)
            for nm, bias, plane in (("w2", "rw_w0_2", 6), ("a2", "rw_a0_2", 7)):
                for c in range(2):
                    job(f"{nm}{c}")
                    ps = wait_filled(act, "acc", f"{nm}{c}")
                    for m in range(4):
                        drain("acc", f"{nm}{c}", pl(plane)[:, 4 * c + m, :], ps[:, m * T:(m + 1) * T], ACT.Sigmoid,
                              last=m == 3, bias=V(bias, 4 * c + m))
            for nm, plane in (("g2", 8), ("r", 9), ("kk", 10)):
                for c in range(2):
                    drain4(f"{nm}{c}", plane, c, ACT.Copy)
            for j in range(4):
                act.wait_ge(S("kk_raw"), 2 * j + 2)
                if j == 0:
                    drain4("vv0", 11, 0, ACT.Copy)
                do(f_(arena[:, 3, 512 * j:512 * (j + 1)], arena[:, 2, 512 * j:512 * (j + 1)], ACT.Square), "kk_sq")
            drain4("vv1", 11, 1, ACT.Copy)
            for j in range(4):
                head_sqrt("kkn", 3, 1.0, 0.0, j)
            for g in range(2):
                for b in range(2):
                    tokens("wt", g, b, tok(0)[:, g, :])
            act.wait_ge(S("cum_ready"), 1)
            do(f_(arena[:, 14, :], arena[:, 12, :], ACT.Exp, scale=-KAPPA), "decays")
            act.wait_ge(S("bonus"), 4)
            do(f_(arena[:, 13, :], arena[:, 12, :], ACT.Exp, scale=KAPPA), "decays")
            act.wait_ge(S("cum_ready"), 2)
            do(f_(arena[:, 6, :], arena[:, 12, :], ACT.Exp, scale=-KAPPA), "decays")

            def turn(name, g, b):
                ps = wait_filled(act, "aux", name)
                drain("aux", name, TI[:, 4 * b:4 * b + 4, :].rearrange("p h t -> p (h t)"), ps[:, :], ACT.Copy)

            for g in range(2):
                for b in range(4):
                    turn(f"t{g}{b}", g, b)
                for nm, dst in (("bt", BTOK), ("kt", KTOK)):
                    for b in range(2):
                        tokens(nm, g, b, dst)
                for lv in range(1, LEVELS + 1):
                    for b in range(4):
                        n = (LEVELS * g + lv - 1) * 4 + b
                        ps = wait_filled(act, "aux", f"u{g}{lv}{b}")
                        drain("aux", f"u{g}{lv}{b}", UU[:, n % 2, :], ps[:, :], ACT.Copy)
                    if lv < LEVELS:
                        for b in range(4):
                            turn(f"t{g}{lv}{b}", g, b)
                for c in range(2):
                    cs = slice(64 * c, 64 * c + 64)
                    n = 2 * g + c
                    for b in range(2):
                        ps = wait_filled(act, "aux", f"x{n}{b}")
                        drain("aux", f"x{n}{b}", XSA[cs, 512 * b:512 * (b + 1)], ps[cs, :], ACT.Copy)
                ps = wait_filled(act, "acc", f"y{g}")
                drain("acc", f"y{g}", pl(7)[:, :, g * P:(g + 1) * P], ps.rearrange("p (f t) -> p f t", t=P)
                      if hasattr(ps, "rearrange") else ps[:, :].rearrange("p (f t) -> p f t", t=P), ACT.Copy)
            for j in range(4):
                act.wait_ge(S("rw_c"), j + 1)
                do(f_(arena[:, 6, 512 * j:512 * (j + 1)], arena[:, 7, 512 * j:512 * (j + 1)], ACT.Square), "rw_sq")
            for j in range(4):
                head_sqrt("wvar", 6, 1.0 / 64, GN_EPS, j)
            for c in range(2):
                job(f"wo{c}")
            norm(4)
            ffn(1)

            norm(5)
            act.dma_start(selm, d["sel"].rearrange("k (h t) -> k h t", t=P)).then_inc(S("sel"), 16)
            act.dma_start(gateb[:, 0:1], d["ml_b_i_2"].rearrange("a h -> h a")).then_inc(S("sel"), 16)
            act.dma_start(gateb[:, 1:2], d["ml_b_f_2"].rearrange("a h -> h a")).then_inc(S("sel"), 16)
            job("gt")
            act.wait_ge(S("gate_b"), 1)
            ps = wait_filled(act, "acc", "gt")
            do(f_(gts[:, 0, :], ps[0:NF, 0:T], ACT.Tanh, scale=1.0 / CAP, bias=gateb[:, 0:1]))
            drain("acc", "gt", gts[:, 1, :], ps[0:NF, T:2 * T], ACT.Tanh, scale=1.0 / CAP, bias=gateb[:, 1:2])
            act.wait_ge(drained("acc", "gt"), acc_jobs["gt"] // 2 + 1)
            do(f_(gts[:, 1, :], gts[:, 1, :], ACT.Exp, scale=-CAP))
            fence()
            do(f_(gts[:, 1, :], gts[:, 1, :], ACT.Ln, bias=1.0), "softplus")
            for nm, plane, func in (("qk", 2, ACT.Copy), ("mv", 4, ACT.Copy), ("o", 5, ACT.Sigmoid)):
                for c in range(2):
                    drain4(f"{nm}{c}", plane, c, func)
            for f in range(NF):
                act.wait_ge(S("ml_conv"), f + 1)
                do(f_(pl(3)[:, f, :], pl(12)[:, f, :], ACT.Silu), "ml_act")
            for g in range(2):
                for b in range(2):
                    tokens("mt", g, b, tok(6)[:, g, :])
            for h in range(NF):
                ps = wait_filled(act, "aux", f"gb{h}")
                act.wait_ge(S("ml_dd"), 2 * h + 2)
                do(f_(dbuf[:, h % 2, :], dbuf[:, h % 2, :], ACT.Exp, scale=-1.0), "ml_de")
                if h >= 2:
                    act.wait_ge(S("ml_y"), h - 1)
                drain("aux", f"gb{h}", ebuf[:, h % 2, :], ps[:, T:2 * T], ACT.Exp)
            for j in range(4):
                act.wait_ge(S("ml_y"), 2 * j + 2)
                do(f_(arena[:, 12, 512 * j:512 * (j + 1)], arena[:, 11, 512 * j:512 * (j + 1)], ACT.Square), "ml_sq")
            for j in range(4):
                head_sqrt("msq", 12, 1.0 / P, EPS, j)
            for c in range(2):
                job(f"lo{c}")
            norm(6)
            ffn(2)
            norm(7)

        @block.gpsimd
        def _(pool):
            for g in range(2):
                for lv in range(1, LEVELS + 1):
                    for b in range(4):
                        n = (LEVELS * g + lv - 1) * 4 + b
                        if lv == 1:
                            pool.wait_ge(S("mm_ready"), 16 * g + 4 * b + 4)
                        if n >= 2:
                            m = n - 2
                            wait_filled(pool, "aux", f"u{m // (4 * LEVELS)}{m // 4 % LEVELS + 1}{m % 4}")
                        pool.tensor_tensor(NM[:, n % 2, :].rearrange("p (h t) -> p h t", t=P),
                                           MM[:, 4 * b:4 * b + 4, 0:P],
                                           bcast(cc(C_LVL + lv * P), 4), ALU.mult)\
                            .then_inc(S("nm_ready"), 1)
            for h in range(NF):
                pool.wait_ge(S("ml_de"), h + 1)
                diag = dbuf[:, h % 2, :].rearrange("p (b t) -> p b t", t=P)[:, 0:3:2, :]
                pool.tensor_tensor(diag, diag, bcast(cc(C_CAUS), 2), ALU.mult).then_inc(S("ml_mask"), 1)

        @block.vector
        def _(dve):
            count = {}

            def do(ins, sig="dve_step"):
                count[sig] = count.get(sig, 0) + 1
                last[0] = sig
                ins.then_inc(S(sig), 1)
                return count[sig]

            last = [None]

            def fence(sig=None):
                dve.wait_ge(S(sig or last[0]), count[sig or last[0]])

            tt, ts, stt = dve.tensor_tensor, dve.tensor_scalar, dve.scalar_tensor_tensor
            cp = dve.tensor_copy
            at = [0]
            n_split, n_ada = [0], [0]

            def pump(upto):
                while at[0] <= min(upto, len(slots) - 1):
                    j = at[0]
                    kind, _, srcs = slots[j]
                    if kind == "split":
                        q = n_split[0]
                        n = sum(s[2] * s[3] for s in srcs)
                        dve.wait_ge(S("w_hi"), q + 1)
                        if q >= 2:
                            dve.wait_ge(*used[q - 2])
                        tt(wlo[:, q % 2, 0:n], ring[:, j % RING, 0:n], whi[:, q % 2, 0:n].bitcast(F32),
                           ALU.subtract).then_inc(S("w_split"), 1)
                        freed[j] = (S("w_split"), q + 1)
                        n_split[0] += 1
                    elif kind == "ada":
                        g, half = n_ada[0] // 2, n_ada[0] % 2
                        cs = silu_c[:, (0 if g < 12 else 8) + KT * half:][:, 0:KT]
                        if g == 0 and half == 0:
                            dve.wait_ge(S("c_ready"), 1)
                        landed(dve, j)
                        if half == 0 and g >= 1:
                            wait_filled(dve, "aux", f"ada{g - 1}")
                        for k in range(KT):
                            w = ring[:, j % RING, k * COLS:(k + 1) * COLS]
                            if half == 0 and k == 0:
                                last_ada[0] = (S("dve_step"), do(ts(adaacc[:, :], w, cs[:, 0:1], None, ALU.mult)))
                                continue
                            dve.wait_ge(*last_ada[0])
                            sig = "dve_step" if k < KT - 1 else ("ada_half", "ada_summed")[half]
                            n = do(stt(out=adaacc[:, :], in0=w, scalar=cs[:, k:k + 1], in1=adaacc[:, :],
                                       op0=ALU.mult, op1=ALU.add), sig)
                            last_ada[0] = (S(sig), n)
                        freed[j] = last_ada[0]
                        n_ada[0] += 1
                    at[0] += 1

            last_ada = [None]

            def ada_finish(g):
                ps = wait_filled(dve, "aux", f"ada{g}")
                l, c = g // 12, 4 * (g % 12)
                b = V("ada_b", c, 4) if l == 0 else V("ada_b_2", 48 * (l - 1) + c, 4)
                tt(mods[:, l, c:c + 4], ps[:, 0:4], b, ALU.add).then_inc(drained("aux", f"ada{g}"), 1)
                ada_done[0] = g

            ada_done = [-1]

            def job(name):
                pump(job_last[name] + 1)

            def done(name):
                for g in after_job[name]:
                    ada_finish(g)

            def mod(l, i, f=0, n=1):
                g = 12 * l + (8 * i + f + n - 1) // 4
                assert g <= ada_done[0], (l, i, g, ada_done[0])
                return mods[:, l, 8 * i + f:8 * i + f + n]

            def mods_ready(l, i):
                g = 12 * l + (8 * i + 7) // 4
                assert g <= ada_done[0]
                wait_drained(dve, "aux", f"ada{g}")

            def to_input(planes, val, f, nhid=None, sig="in_ready"):
                hi, lo = planes
                n = do(cp(hi, val))
                dve.wait_ge(S("dve_step"), n)
                do(tt(lo, val, hi.bitcast(F32), ALU.subtract), sig)

            def plane_input(planes, plane):
                for f in range(NF):
                    to_input((plr(planes[0])[:, f, :], plr(planes[1])[:, f, :]), pl(plane)[:, f, :], f)
                fence()

            def norm_scale(i):
                wait_drained(dve, "aux", f"norm{i}")
                do(dve.reciprocal(rs[:, :], rs[:, :]))
                fence()

            def norm_mod(i, l, which, gain, val, planes, sig="in_ready"):
                mods_ready(l, 3 * which + 1)
                sc, sh = mod(l, 3 * which + 1, 0, NF), 3 * which
                if gain:
                    do(stt(out=nscale[:, :], in0=sc, scalar=1.0, in1=V(gain, 0, NF), op0=ALU.add, op1=ALU.mult))
                else:
                    do(ts(nscale[:, :], sc, 1.0, None, ALU.add))
                norm_scale(i)
                for f in range(NF):
                    do(stt(out=pl(val)[:, f, :], in0=X[:, f, :], scalar=nscale[:, f:f + 1], in1=rs[:, :],
                           op0=ALU.mult, op1=ALU.mult))
                    fence()
                    do(ts(pl(val)[:, f, :], pl(val)[:, f, :], mod(l, sh, f), None, ALU.add))
                    fence()
                    if planes:
                        to_input((plr(planes[0])[:, f, :], plr(planes[1])[:, f, :]), pl(val)[:, f, :], f)

            def head_center(name, plane, n, sig):
                for j in range(4):
                    ps = wait_filled(dve, "aux", f"{name}mean{j}")
                    y = arena[:, plane, 512 * j:512 * (j + 1)]
                    stt(out=y, in0=ps[:, :], scalar=-1.0 / n, in1=y, op0=ALU.mult, op1=ALU.add)\
                        .then_inc(drained("aux", f"{name}mean{j}"), 1)

            def head_scale(name, plane, sqp):
                for j in range(4):
                    sl = slice(512 * j, 512 * (j + 1))
                    wait_drained(dve, "aux", f"{name}{j}")
                    do(dve.reciprocal(arena[:, sqp, sl], arena[:, sqp, sl]))
                    fence()
                    do(tt(arena[:, plane, sl], arena[:, plane, sl], arena[:, sqp, sl], ALU.mult))

            def update_x(name, l, i):
                for c in range(2):
                    job(f"{name}{c}")
                    ps = wait_filled(dve, "acc", f"{name}{c}")
                    for m in range(4):
                        f = 4 * c + m
                        do(stt(out=X[:, f, :], in0=ps[:, m * T:(m + 1) * T], scalar=mod(l, i, f), in1=X[:, f, :],
                               op0=ALU.mult, op1=ALU.add), "x_ready")
                    do(dve.nop(), "x") if False else None
                    dve_drained(f"{name}{c}")
                    done(f"{name}{c}")

            def dve_drained(name):
                dve.wait_ge(S("x_ready"), count["x_ready"])
                dve.sem_inc(drained("acc", name), 1)

            def ffn(l, ml, mw):
                for c, n in enumerate(FW):
                    job(f"fg{l}{c}")
                    done(f"fg{l}{c}")
                    job(f"fu{l}{c}")
                    wait_drained(dve, "acc", f"fg{l}{c}")
                    ps = wait_filled(dve, "acc", f"fu{l}{c}")
                    pr = prod[:, c % 2, 0:n // P, :]
                    tt(pr.rearrange("p m t -> p (m t)"), ps[:, 0:2 * n],
                       silug[:, c % 2, 0:n // P, :].rearrange("p m t -> p (m t)"), ALU.mult)\
                        .then_inc(drained("acc", f"fu{l}{c}"), 1)
                    wait_drained(dve, "acc", f"fu{l}{c}")
                    o = slice(4 * c, 4 * c + n // P)
                    k = do(cp(hid(HID_HI)[:, o, :], pr), "prod_ready")
                    dve.wait_ge(S("prod_ready"), k)
                    for m in range(n // P):
                        do(tt(hid(HID_LO)[:, 4 * c + m, :], pr[:, m, :],
                              hid(HID_HI)[:, 4 * c + m, :].bitcast(F32), ALU.subtract), "in_ready")
                    done(f"fu{l}{c}")
                update_x(f"fd{l}", ml, mw)

            def skip(names):
                for n in names:
                    job(n)
                    done(n)

            pump(7)
            dve.wait_ge(S("consts"), 32)
            for g in range(4):
                pass
            dve.wait_ge(S("tables"), 32)
            wait_filled(dve, "aux", "norm0")
            scr = pl(14)
            do(cp(scr[:, 0, :], posi))
            fence()
            do(ts(scr[:, 0, :], scr[:, 0, :], cc(C_FREQ, 1), None, ALU.mult))
            fence()
            for r, quarter in ((2, 0.0), (3, 0.25)):
                n = scr[:, 1, :]
                do(ts(n, scr[:, 0, :], float(1 / (2 * np.pi)), quarter, ALU.mult, ALU.add))
                fence()
                do(ts(n, n, 12582912.0, None, ALU.add))
                fence()
                do(ts(n, n, 12582912.0, None, ALU.subtract))
                fence()
                src = scr[:, 0, :]
                for part in TWO_PI:
                    do(stt(out=scr[:, r, :], in0=n, scalar=-part, in1=src, op0=ALU.mult, op1=ALU.add))
                    fence()
                    src = scr[:, r, :]
                if quarter:
                    do(ts(src, src, float(np.pi / 2), None, ALU.add))
                    fence()
                do(ts(src, src, 3.1415925, -3.1415925, ALU.min, ALU.max), "angles")
            for g in range(4):
                ada_finish_or_wait(g) if False else ada_finish(g)
            norm_mod(0, 0, 0, "norm_mix_g", 13, A_IN)
            dve.wait_ge(S("trig"), 2)
            do(ts(sinb, sinb, cc(C_FREQ + 1, 1), None, ALU.mult))
            fence()

            def rope(plane, nm):
                for c in range(2):
                    wait_drained(dve, "acc", f"{nm}{c}")
                t, tmp = pl(plane), pl(14)
                for a, b in ((slice(0, 64), slice(64, 128)), (slice(64, 128), slice(0, 64))):
                    do(tt(tmp[a, :, :], t[b, :, :], bcast(sinb[b, :], NF), ALU.mult))
                fence()
                do(tt(t, t, bcast(cosb, NF), ALU.mult))
                fence()
                do(tt(t, t, tmp, ALU.add), "roped")
                fence("roped")

            skip(["q0", "q1", "k0"])
            rope(2, "q")
            skip(["k1", "v0"])
            rope(3, "k")
            skip(["v1", "g0", "g1"])
            for g in range(2):
                for b in range(2):
                    ps = wait_filled(dve, "aux", f"vt{g}{b}")
                    cp(tok(5)[:, g, 512 * b:512 * (b + 1)], ps[:, :]).then_inc(drained("aux", f"vt{g}{b}"), 1)
            skip(["b0", "b1"])

            def ret_weights(h):
                ps = wait_filled(dve, "aux", f"rs{h}")
                if h >= 2:
                    wait_filled(dve, "aux", f"ry{h - 2}")
                tt(pbuf[:, h % 2, :], ps[:, 0:384], dec[:, h, :], ALU.mult).then_inc(drained("aux", f"rs{h}"), 1)
                wait_drained(dve, "aux", f"rs{h}")
                dve.sem_inc(S("ret_w"), 1)

            ret_weights(0)
            ret_weights(1)
            for n in range(4):
                nm = f"c{n}" if n < 2 else f"u{n - 2}"
                job(nm)
                if n >= 2:
                    c = n - 2
                    ps = wait_filled(dve, "acc", nm)
                    wait_drained(dve, "acc", f"c{c}")
                    o = arena[:, 8, 1024 * c:1024 * (c + 1)]
                    tt(o, ps[:, :], o, ALU.mult).then_inc(drained("acc", nm), 1)
                done(nm)
                if n < 3:
                    ret_weights(2 * n + 2)
                    ret_weights(2 * n + 3)
            job("ga0")
            done("ga0")
            for h in range(NF):
                wait_drained(dve, "aux", f"ry{h}")
            dve.sem_inc(S("ry_all"), 4)
            head_center("r", 13, P, "ret_c")
            for j in range(4):
                wait_drained(dve, "aux", f"rmean{j}")
                dve.sem_inc(S("ret_c"), 1)
            job("ga1")
            done("ga1")
            for c in range(2):
                wait_drained(dve, "acc", f"u{c}")
                wait_drained(dve, "acc", f"b{c}")
            u, cv = pl(8), pl(5)
            for f in range(NF):
                do(ts(cv[:, f, :], u[:, f, :], V("conv_w", 16 + f), None, ALU.mult))
                fence()
                for tap, back in ((1, 1), (0, 2)):
                    do(stt(out=cv[:, f, back:T], in0=u[:, f, 0:T - back], scalar=V("conv_w", 8 * tap + f),
                           in1=cv[:, f, back:T], op0=ALU.mult, op1=ALU.add))
                    fence()
                do(tt(pl(7)[:, f, :], pl(7)[:, f, :], cv[:, f, :], ALU.mult))
                fence()
                to_input((plr(2)[:, f, :], plr(3)[:, f, :]), pl(7)[:, f, :], f)
            job("gb0")
            done("gb0")
            head_scale("rvar", 13, 14)
            fence()
            do(tt(arena[:, 6, :], arena[:, 6, :], arena[:, 13, :], ALU.mult))
            fence()
            job("gb1")
            done("gb1")
            wait_filled(dve, "acc", "gb1")
            plane_input(A_IN, 6)
            for c in range(2):
                job(f"co{c}")
                wait_drained(dve, "acc", f"gb{c}")
                ps = wait_filled(dve, "acc", f"co{c}")
                tt(arena[:, 8, 1024 * c:1024 * (c + 1)], ps[:, :], arena[:, 10, 1024 * c:1024 * (c + 1)], ALU.mult)\
                    .then_inc(drained("acc", f"co{c}"), 1)
                done(f"co{c}")
            for c in range(2):
                job(f"ro{c}")
                ps = wait_filled(dve, "acc", f"ro{c}")
                wait_drained(dve, "acc", f"ga{c}") if False else None
                o = arena[:, 9, 1024 * c:1024 * (c + 1)]
                tt(o, ps[:, :], o, ALU.mult).then_inc(drained("acc", f"ro{c}"), 1)
                wait_drained(dve, "acc", f"ro{c}")
                wait_drained(dve, "acc", f"co{c}")
                do(tt(o, o, arena[:, 8, 1024 * c:1024 * (c + 1)], ALU.add))
                fence()
                for f in range(4 * c, 4 * c + 4):
                    to_input((plr(2)[:, f, :], plr(3)[:, f, :]), pl(9)[:, f, :], f)
                done(f"ro{c}")
            update_x("mo", 0, 2)
            norm_mod(1, 0, 1, "norm_ffn_g", 13, A_IN)
            ffn(0, 0, 5)
            norm_scale(2)
            for f in range(NF):
                do(stt(out=X[:, f, :], in0=X[:, f, :], scalar=V("final_norm_g", f), in1=rs[:, :], op0=ALU.mult,
                       op1=ALU.mult), "x_ready")

            norm_mod(3, 1, 0, None, 2, None)
            hf, xx = pl(2), pl(3)
            do(tt(xx[:, :, 1:T], hf[:, :, 0:T - 1], hf[:, :, 1:T], ALU.subtract))
            do(ts(xx[:, :, 0:1], hf[:, :, 0:1], -1.0, None, ALU.mult))
            fence()

            def mixed(i, plane, sig="in_ready"):
                for f in range(NF):
                    do(stt(out=pl(plane)[:, f, :], in0=xx[:, f, :], scalar=V("rw_mix_2", 8 * i + f), in1=hf[:, f, :],
                           op0=ALU.mult, op1=ALU.add), sig)

            mixed(1, 0)
            mixed(4, 1)
            mixed(5, 4)
            mixed(0, 13, "dve_step")
            fence()
            skip(["wl", "al"])
            wait_filled(dve, "acc", "al")
            plane_input((0, 1), 13)
            mixed(2, 13, "dve_step")
            fence()
            skip(["gl"])
            wait_filled(dve, "acc", "gl")
            plane_input((4, 5), 13)
            mixed(3, 13, "dve_step")
            fence()
            skip(["w20", "w21", "a20", "a21", "g20", "g21"])
            for c in range(2):
                wait_drained(dve, "acc", f"w2{c}")
            wait_filled(dve, "acc", "g21")
            ld, cum = pl(6), pl(12)
            for f in range(NF):
                for n in range(4):
                    sl = slice(64 * n, 64 * n + 64)
                    do(dve.tensor_tensor_scan(cum[:, f, sl], ld[:, f, sl], cst[:, C_ZERO:C_ZERO + 64], 0.0,
                                              ALU.add, ALU.add))
            skip(["r0"])
            do(dve.nop(), "dve_step") if False else None
            fence()
            dve.sem_inc(S("cum_ready"), 1)
            skip(["r1"])
            wait_filled(dve, "acc", "r1")
            plane_input((0, 1), 13)
            skip(["kk0", "kk1"])
            for c in range(2):
                wait_drained(dve, "acc", f"kk{c}")
                wait_drained(dve, "acc", f"a2{c}")
                wait_drained(dve, "acc", f"r{c}")
            for f in range(NF):
                do(ts(pl(2)[:, f, :], pl(10)[:, f, :], V("rw_k_k_2", f), None, ALU.mult), "kk_raw")
            job("vv0")
            for f in range(NF):
                do(ts(pl(13)[:, f, :], pl(7)[:, f, :], 1.0, V("rw_k_a_2", f), ALU.subtract, ALU.mult))
            fence()
            do(stt(out=arena[:, 10, :], in0=arena[:, 13, :], scalar=1.0, in1=arena[:, 10, :], op0=ALU.add,
                   op1=ALU.mult))
            fence()
            done("vv0")
            job("vv1")
            for f in range(NF):
                do(stt(out=pl(13)[:, f, :], in0=pl(9)[:, f, :], scalar=V("rw_r_k_2", f), in1=pl(10)[:, f, :],
                       op0=ALU.mult, op1=ALU.mult))
            fence()
            dve.sem_inc(S("rk_ready"), 4)
            done("vv1")
            for j in range(4):
                sl = slice(512 * j, 512 * (j + 1))
                wait_drained(dve, "aux", f"kkn{j}")
                do(ts(arena[:, 3, sl], arena[:, 3, sl], 1e-12, None, ALU.max))
                fence()
                do(dve.reciprocal(arena[:, 3, sl], arena[:, 3, sl]))
                fence()
                do(tt(arena[:, 2, sl], arena[:, 2, sl], arena[:, 3, sl], ALU.mult))
            for c in range(2):
                wait_drained(dve, "acc", f"vv{c}")
            wait_filled(dve, "acc", "vv1")
            for j in range(4):
                sl = slice(512 * j, 512 * (j + 1))
                ps = wait_filled(dve, "aux", f"bon{j}")
                tt(arena[:, 1, sl], ps[:, :], arena[:, 11, sl], ALU.mult).then_inc(drained("aux", f"bon{j}"), 1)
            wait_drained(dve, "aux", "bon3")
            dve.sem_inc(S("bonus"), 4)
            dve.wait_ge(S("decays"), 2)
            do(cp(pend[:, :, :], pl(14)[:, :, 63::64]))
            do(tt(arena[:, 12, :], arena[:, 12, :], arena[:, 6, :], ALU.subtract))
            fence()
            dve.sem_inc(S("cum_ready"), 1)
            do(tt(arena[:, 7, :], arena[:, 7, :], arena[:, 2, :], ALU.mult))
            fence()
            do(tt(arena[:, 7, :], arena[:, 7, :], arena[:, 13, :], ALU.mult), "hats")
            do(tt(arena[:, 10, :], arena[:, 10, :], arena[:, 13, :], ALU.mult), "hats")
            for g in range(2):
                gs = slice(g * P, (g + 1) * P)
                do(tt(AR[:, :, g, 1, :], pl(9)[:, :, gs], pl(14)[:, :, gs], ALU.mult), "hats")
            dve.wait_ge(S("decays"), 3)
            for g in range(2):
                gs = slice(g * P, (g + 1) * P)
                do(stt(out=AR[:, :, g, 0, :], in0=pl(2)[:, :, gs], scalar=-1.0, in1=pl(6)[:, :, gs], op0=ALU.mult,
                       op1=ALU.mult), "hats")
            fence("hats")
            do(dve.memset(state[:, :, :], 0.0))
            fence()
            dve.sem_inc(S("state_ready"), 4)
            for g in range(2):
                for h in range(16):
                    ps = wait_filled(dve, "aux", f"m{g}{h}")
                    if h == 0:
                        if g == 0:
                            for gg in range(2):
                                for bb in range(2):
                                    wait_drained(dve, "aux", f"wt{gg}{bb}")
                        else:
                            wait_filled(dve, "acc", "y0")
                    tt(MM[:, h, :].rearrange("p (a t) -> p a t", a=2), ps[:, :].rearrange("p (a t) -> p a t", a=2),
                       bcast(cc(C_MASK, 256), 2), ALU.mult).then_inc(drained("aux", f"m{g}{h}"), 1)
                    if h % 4 == 3:
                        b = h // 4
                        wait_drained(dve, "aux", f"m{g}{h}")
                        dve.sem_inc(S("mm_ready"), 4)
                        sl = slice(4 * b, 4 * b + 4)
                        do(tt(TT[:, sl, :], MM[:, sl, 0:P], bcast(cc(C_LVL), 4), ALU.mult))
                        fence()
                        do(tt(TT[:, sl, :], TT[:, sl, :], bcast(ident, 4), ALU.add), "tt_ready")
                for lv in range(1, LEVELS + 1):
                    for b in range(4):
                        sl = slice(4 * b, 4 * b + 4)
                        ps = wait_filled(dve, "aux", f"v{g}{lv}{b}")
                        t = TT[:, sl, :].rearrange("p h t -> p (h t)")
                        if lv == 1:
                            fence("tt_ready")
                        tt(t, ps[:, :], t, ALU.add).then_inc(drained("aux", f"v{g}{lv}{b}"), 1)
                count["tt_ready"] += 0
                dve.sem_inc(S("tt_ready"), 4 * LEVELS)
                count["tt_ready"] += 4 * LEVELS
                for c in range(2):
                    cs = slice(64 * c, 64 * c + 64)
                    n = 2 * g + c
                    for b in range(2):
                        ps = wait_filled(dve, "aux", f"sa{n}{b}")
                        cp(SAT[cs, 512 * b:512 * (b + 1)], ps[cs, :]).then_inc(drained("aux", f"sa{n}{b}"), 1)
                    for b in range(2):
                        ps = wait_filled(dve, "aux", f"st{n}{b}")
                        for i in range(2):
                            rr = slice(64 * i, 64 * i + 64)
                            s = state[rr, 4 * b:4 * b + 4, 64 * i:64 * i + 64]
                            ins = tt(s, ps[rr, :].rearrange("p (f v) -> p f v", v=P)[:, :, 64 * i:64 * i + 64], s,
                                     ALU.add)
                            if i == 1:
                                ins.then_inc(drained("aux", f"st{n}{b}"), 1)
                                wait_drained(dve, "aux", f"st{n}{b}")
                            else:
                                do(ins)
                        for i in range(2):
                            rr = slice(64 * i, 64 * i + 64)
                            s = state[rr, 4 * b:4 * b + 4, 64 * i:64 * i + 64]
                            do(tt(s, s, pend[rr, 4 * b:4 * b + 4, n:n + 1].to_broadcast([64, 4, 64]), ALU.mult))
                    fence()
                    dve.sem_inc(S("state_ready"), 4)
            wait_drained(dve, "acc", "y1")
            wait_drained(dve, "acc", "y0")
            dve.sem_inc(S("wy_all"), 4)
            head_center("w", 7, 64, "rw_c")
            for j in range(4):
                wait_drained(dve, "aux", f"wmean{j}")
                dve.sem_inc(S("rw_c"), 1)
            head_scale("wvar", 7, 6)
            fence()
            for f in range(NF):
                y = pl(7)[:, f, :]
                do(ts(y, y, V("rw_gn_w_2", f), V("rw_gn_b_2", f), ALU.mult, ALU.add))
                fence()
                do(tt(y, y, pl(1)[:, f, :], ALU.add))
                fence()
                do(tt(y, y, pl(8)[:, f, :], ALU.mult))
                fence()
                to_input((plr(4)[:, f, :], plr(5)[:, f, :]), y, f)
            update_x("wo", 1, 2)
            norm_mod(4, 1, 1, None, 13, A_IN)
            ffn(1, 1, 5)

            norm_mod(5, 2, 0, None, 13, A_IN)
            dve.wait_ge(S("sel"), 48)
            do(ts(gateb[:, :], gateb[:, :], 1.0 / CAP, None, ALU.mult), "gate_b")
            skip(["gt"])
            dve.wait_ge(S("softplus"), 1)
            G = lambda i: gts[:, i, :]
            do(dve.memset(G(6), 0.0))
            fence()
            do(dve.tensor_tensor_scan(G(2), G(1), G(6), 0.0, ALU.add, ALU.add))
            fence()
            do(stt(out=G(3), in0=G(0), scalar=CAP, in1=G(2), op0=ALU.mult, op1=ALU.add))
            fence()
            do(dve.tensor_tensor_scan(G(4), G(3), G(3), 0.0, ALU.max, ALU.max))
            fence()
            do(tt(G(5), G(2), G(4), ALU.subtract), "gates")
            fence("gates")
            dve.sem_inc(S("gates"), 1)
            skip(["qk0", "qk1", "mv0"])
            for c in range(2):
                wait_drained(dve, "acc", f"qk{c}")
            for f in range(NF):
                x, y = pl(2)[:, f, :], pl(12)[:, f, :]
                do(ts(y, x, V("ml_conv_w_2", 24 + f), V("ml_conv_b_2", f), ALU.mult, ALU.add))
                for tap, back in ((2, 1), (1, 2), (0, 3)):
                    fence()
                    do(stt(out=y[:, back:T], in0=x[:, 0:T - back], scalar=V("ml_conv_w_2", 8 * tap + f),
                           in1=y[:, back:T], op0=ALU.mult, op1=ALU.add), "ml_conv" if tap == 0 else "dve_step")
                if f == 3:
                    skip(["mv1"])
            skip(["o0", "o1"])
            ps = wait_filled(dve, "aux", "ut")
            cp(ucol, ps[:, 0:16]).then_inc(drained("aux", "ut"), 1)
            wait_drained(dve, "aux", "ut")

            def ml_out(h):
                ps = wait_filled(dve, "aux", f"nd{h}")
                wait_drained(dve, "aux", f"gb{h}")
                dn = ebuf[:, 2 + h % 2, :]
                do(stt(out=dn, in0=ps[:, T:2 * T], scalar=-1.0, in1=ebuf[:, h % 2, :], op0=ALU.mult, op1=ALU.max))
                fence()
                do(tt(dn, ps[:, T:2 * T], dn, ALU.max))
                fence()
                do(dve.reciprocal(dn, dn))
                fence()
                tt(pl(11)[:, h, :], ps[:, 0:T], dn, ALU.mult).then_inc(drained("aux", f"nd{h}"), 1)
                wait_drained(dve, "aux", f"nd{h}")
                dve.sem_inc(S("ml_y"), 1)

            for h in range(NF):
                ps = wait_filled(dve, "aux", f"gb{h}")
                dd = dbuf[:, h % 2, :]
                do(ts(dd[:, 0:T], ps[:, 0:T], ucol[:, h:h + 1], 0.0, ALU.subtract, ALU.max), "ml_dd")
                do(ts(dd[:, T:384], ps[:, P:T], ucol[:, NF + h:NF + h + 1], 0.0, ALU.subtract, ALU.max), "ml_dd")
                ps = wait_filled(dve, "aux", f"ms{h}")
                dve.wait_ge(S("ml_mask"), h + 1)
                if h >= 2:
                    wait_filled(dve, "aux", f"nd{h - 2}")
                stt(out=dbuf[:, 3 + h % 2, :], in0=ps[:, 0:384], scalar=64 ** -0.5, in1=dbuf[:, h % 2, :], op0=ALU.mult,
                    op1=ALU.mult).then_inc(drained("aux", f"ms{h}"), 1)
                wait_drained(dve, "aux", f"ms{h}")
                dve.sem_inc(S("ml_w"), 1)
                if h >= 1:
                    ml_out(h - 1)
            ml_out(NF - 1)
            head_scale("msq", 11, 12)
            fence()
            for c in range(2):
                wait_drained(dve, "acc", f"o{c}")
            for f in range(NF):
                y = pl(11)[:, f, :]
                do(stt(out=y, in0=y, scalar=V("ml_hn_w_2", f), in1=pl(5)[:, f, :], op0=ALU.mult, op1=ALU.mult))
                fence()
                to_input((plr(0)[:, f, :], plr(1)[:, f, :]), y, f)
            update_x("lo", 2, 2)
            norm_mod(6, 2, 1, None, 13, A_IN)
            ffn(2, 2, 5)
            norm_scale(7)
            for f in range(NF):
                do(stt(out=pl(0)[:, f, :], in0=X[:, f, :], scalar=V("final_w_2", f), in1=rs[:, :], op0=ALU.mult,
                       op1=ALU.mult), "y_out")

        @block.sync
        def _(sp):
            for j, (kind, _, srcs) in enumerate(slots):
                if j >= RING:
                    sp.wait_ge(*freed[j - RING])
                for rws, c0, n, ncols, src in srcs:
                    sp.dma_start(ring[0:rws, j % RING, c0:c0 + n * ncols].rearrange("p (k n) -> p k n", n=ncols), src)\
                        .then_inc(S(f"w_landed{j % RING}"), 16)
            for h in range(2):
                sp.wait_ge(S("y_out"), 4 * h + 4)
                sp.dma_start(d["out"][:, 4 * h:4 * h + 4, :], pl(0)[:, 4 * h:4 * h + 4, :]).then_inc(S("stored"), 16)
            sp.wait_ge(S("stored"), 32)


_VEC_NAMES = [n for n, _ in VECS]
_BIG = ["positions", "ada_w", "w_in", "ret_w_out", "conv_w_out", "mix_w_out", "ffn_w_gate", "ffn_w_up", "ffn_w_down",
        "ada_w_2", "rw_w_in_2", "rw_w2_2", "rw_a2_2", "rw_g2_2", "rw_w_out_2", "ml_w_in_2", "ml_b_i_2", "ml_b_f_2",
        "ml_w_out_2", "ffn_w_gu_2", "ffn_w_down_2"]


def kernel(**inputs):
    import concourse.bacc as bacc
    from concourse.bass_utils import run_bass_kernel_spmd

    nc = bacc.Bacc("TRN2", target_bir_lowering=False, num_devices=1)
    arrays = {n: np.ascontiguousarray(inputs[n]) for n in _BIG}
    arrays["x"] = np.ascontiguousarray(np.asarray(inputs["x"]).reshape(T, NF, P).transpose(2, 1, 0))
    arrays["vec"] = np.ascontiguousarray(
        np.concatenate([np.asarray(inputs[n]).reshape(-1, P) for n in _VEC_NAMES], 0).T)
    arrays["cst"], arrays["dec"], arrays["sel"] = shape_constants()
    d = {}
    for n, a in arrays.items():
        d[n] = nc.dram_tensor(f"in_{n}", a.shape, mybir.dt.from_np(a.dtype), kind="ExternalInput").ap()
    d["out"] = nc.dram_tensor("out_y", (P, NF, T), F32, kind="ExternalOutput").ap()
    build(nc, d)
    r = run_bass_kernel_spmd(nc, [{f"in_{n}": a for n, a in arrays.items()}], core_ids=[0])
    y = r.results[0]["out_y"]
    return np.ascontiguousarray(y.transpose(2, 1, 0)).reshape(1, T, D)
```

```python
from contextlib import ExitStack

import concourse.bass as bass
import numpy as np
from concourse import mybir

F32 = mybir.dt.float32
F32R = mybir.dt.float32r
I32 = mybir.dt.int32
ALU = mybir.AluOpType
ACT = mybir.ActivationFunctionType

P = 128
D = 1024
T = 256
NF = D // P
PLANE = NF * T
FFN = 2816
NH = FFN // P
EPS = 1e-6
GN_EPS = 64e-5
KAPPA = float(np.exp(-0.5))
CH = 64
LEVELS = 5
CAP = 15.0

RING = 4
KT = 4
COLS = 512
SLOT = KT * COLS
NPLANES = 15

C_ID, C_ONE, C_BLK, C_MASK, C_LVL = 0, 128, 256, 384, 640
C_CAUS = C_LVL + 128 * (LEVELS + 1)
C_FREQ = C_CAUS + P
C_ZERO = C_FREQ + 2
NCONST = C_ZERO + 64
TWO_PI = (6.28125, 0.0019350051879882812, 3.019916050561733e-07)

VECS = [("c", 8), ("c_2", 8), ("ada_b", 48), ("ada_b_2", 96), ("norm_mix_g", 8), ("norm_ffn_g", 8),
        ("final_norm_g", 8), ("conv_w", 24), ("rw_mix_2", 48), ("rw_w0_2", 8), ("rw_a0_2", 8), ("rw_k_k_2", 8),
        ("rw_k_a_2", 8), ("rw_r_k_2", 8), ("rw_gn_w_2", 8), ("rw_gn_b_2", 8), ("ml_conv_w_2", 32),
        ("ml_conv_b_2", 8), ("ml_hn_w_2", 8), ("final_w_2", 8)]
VOFF = {}
_n = 0
for _name, _w in VECS:
    VOFF[_name] = _n
    _n += _w
NVEC = _n


def shape_constants():
    c = np.zeros((P, NCONST), np.float32)
    i = np.arange(P)
    s, t = i[:, None], i[None, :]
    c[:, C_ID:C_ID + P] = s == t
    c[:, C_ONE:C_ONE + P] = 1.0
    c[:, C_BLK:C_BLK + P] = s // 64 == t // 64
    same = s // CH == t // CH
    strict, incl = same & (s < t), same & (s <= t)
    c[:, C_MASK:C_MASK + 256] = np.concatenate([strict, incl], 1)
    for lv in range(LEVELS + 1):
        half = 1 << lv
        off = (s // (2 * half) == t // (2 * half)) & (s % (2 * half) < half) & (t % (2 * half) >= half)
        c[:, C_LVL + lv * P:C_LVL + (lv + 1) * P] = off
    c[:, C_CAUS:C_CAUS + P] = s <= t
    c[:, C_FREQ] = 1.0 / (np.float32(10000.0) ** (np.arange(0, P, 2, dtype=np.float32) / np.float32(P)))[i % 64]
    c[:, C_FREQ + 1] = np.where(i < 64, 1.0, -1.0)
    h = np.arange(NF, dtype=np.float32)
    lg = np.log(1.0 - 2.0 ** (-5.0 - h.astype(np.float64)))
    rel = np.arange(T)[None, :] - s
    dec = np.where(rel[:, None, :] >= 0, np.exp(lg[None, :, None] * np.maximum(rel, 0)[:, None, :]), 0.0) * P ** -0.5
    dec = np.concatenate([dec, dec[:, :, 0:P]], 2).astype(np.float32).reshape(P, NF * 384)
    sel = np.zeros((NF, NF, P), np.float32)
    for k in range(NF):
        sel[k, k, :] = 1.0
    return c, dec, sel.reshape(NF, NF * P)


def build(nc, d):
    ctx = ExitStack()
    with ctx:
        def sb(name, shape, dt=F32):
            return ctx.enter_context(nc.sbuf_tensor(name, shape, dt))

        sems = {}

        def S(name):
            if name not in sems:
                sems[name] = ctx.enter_context(nc.semaphore(name))
            return sems[name]

        ring = sb("ring", [P, RING, SLOT])
        whi = sb("whi", [P, 2, SLOT], F32R)
        wlo = sb("wlo", [P, 2, SLOT], F32R)
        X = sb("X", [P, NF, T])
        cst = sb("cst", [P, NCONST])
        vec = sb("vec", [P, NVEC])
        mods = sb("mods", [P, 3, 48])
        silu_c = sb("silu_c", [P, 16])
        nscale = sb("nscale", [P, NF])
        gateb = sb("gateb", [NF, 2])
        tiny = sb("tiny", [P, 1])
        adaacc = sb("adaacc", [P, COLS])
        rs = sb("rs", [P, T])
        state = sb("state", [P, NF, P])
        pend = sb("pend", [P, NF, 4])
        parts_r = {}
        for first, n in ((0, 1), (1, 1), (2, 1), (3, 1), (4, 1), (5, 1), (2, 3), (5, 3)):
            with ExitStack() as at_plane:
                if first:
                    at_plane.enter_context(nc.sbuf_tensor(f"below{first}_{n}", [P, first, PLANE], F32))
                parts_r[first, n] = at_plane.enter_context(nc.sbuf_tensor(f"parts{first}_{n}", [P, n, PLANE], F32R))
        arena = sb("arena", [P, NPLANES, PLANE])

        acc = [ctx.enter_context(nc.psum_tensor(f"acc{b}", [P, 1024], F32)) for b in range(2)]
        aux = [ctx.enter_context(nc.psum_tensor(f"aux{b}", [P, 512], F32)) for b in range(4)]

        def pl(i):
            return arena[:, i, :].rearrange("p (f t) -> p f t", t=T)

        def plr(i):
            return parts_r[i, 1][:, 0, :].rearrange("p (f t) -> p f t", t=T)

        def bcast(ap, n):
            return ap.rearrange("p (a t) -> p a t", a=1).to_broadcast([ap.shape[0], n, ap.shape[1]])

        def cc(o, n=P):
            return cst[:, o:o + n]

        def V(name, i=0, n=1, rows=P):
            return vec[0:rows, VOFF[name] + i:VOFF[name] + i + n]

        ident, ones, blk = cc(C_ID), cc(C_ONE), cc(C_BLK)

        block = ctx.enter_context(nc.Block())

        acc_jobs, aux_jobs = {}, {}

        def wait_filled(e, kind, name):
            a, n = (acc_jobs, 2) if kind == "acc" else (aux_jobs, 4)
            a = a[name]
            e.wait_ge(S(f"{kind}_filled{a % n}"), a // n + 1)
            return (acc if kind == "acc" else aux)[a % n]

        def drained(kind, name):
            a, n = (acc_jobs, 2) if kind == "acc" else (aux_jobs, 4)
            return S(f"{kind}_drained{a[name] % n}")

        def wait_drained(e, kind, name):
            a, n = (acc_jobs, 2) if kind == "acc" else (aux_jobs, 4)
            a = a[name]
            e.wait_ge(S(f"{kind}_drained{a % n}"), a // n + 1)


        slots = []
        freed = {}
        split_of, used, hi_used = [], [], []
        ada_slots = []
        job_last = {}
        after_job = {}

        def add_slot(kind, dst, srcs):
            slots.append((kind, dst, srcs))
            return len(slots) - 1

        def landed(e, j):
            n = sum(len(slots[i][2]) for i in range(j % RING, j + 1, RING))
            e.wait_ge(S(f"w_landed{j % RING}"), 16 * n)

        def rows_of(w, k0, n, c0, ncols):
            return (P, 0, n, ncols, w[k0 * P:(k0 + n) * P, c0:c0 + ncols].rearrange("(k p) n -> p k n", p=P))

        def ada_half():
            g, half = len(ada_slots) // 2, len(ada_slots) % 2
            if g < 36:
                w = (d["ada_w"][0], d["ada_w_2"][0], d["ada_w_2"][1])[g // 12]
                ada_slots.append(add_slot("ada", None, [rows_of(w, KT * half, KT, (g % 12) * COLS, COLS)]))

        def ahead(name, n):
            j, n_split, n_ada = job_last[name], 0, 0
            while j + 1 < len(slots) and n_split < n:
                kind = slots[j + 1][0]
                if kind == "ada" and n_ada == 1:
                    break
                n_split += kind == "split"
                n_ada += kind == "ada"
                j += 1
            return j

        N_FIRST = 4

        def ada_sum(g):
            return arena[:, 10, COLS * g:COLS * (g + 1)] if g < N_FIRST else adaacc[:, :]

        A_IN, B_IN = (0, 1), (2, 3)
        HID_HI, HID_LO = 2, 5
        AR = arena[:, 4:6, :].rearrange("p a n -> p (a n)").rearrange("p (f g r t) -> p f g r t", f=NF, g=2, r=2)
        MM = arena[:, 11:15, :].rearrange("p a n -> p (a n)").rearrange("p (h q) -> p h q", q=512)
        TI = arena[:, 2, :].rearrange("p (h t) -> p h t", t=P)
        TT = arena[:, 3, :].rearrange("p (h t) -> p h t", t=P)
        NM = arena[:, 1, 0:1024].rearrange("p (b n) -> p b n", n=512)
        UU = arena[:, 1, 1024:2048].rearrange("p (b n) -> p b n", n=512)
        BTOK, KTOK = arena[:, 9, 0:1024], arena[:, 9, 1024:2048]
        XSA = arena[:, 2, 0:1024]
        SAT = arena[:, 2, 1024:2048]
        dec = arena[:, 11:13, :].rearrange("p a n -> p (a n)")[:, 0:NF * 384].rearrange("p (h t) -> p h t", t=384)
        cosb, sinb = arena[:, 12, 1024:1280], arena[:, 12, 1280:1536]
        posi = arena[:, 12, 1536:1792].bitcast(I32)
        pbuf = arena[:, 4, 0:768].rearrange("p (b t) -> p b t", t=384)
        lora = state[:, :, :].rearrange("p f v -> p (f v)").rearrange("p (b t) -> p b t", t=T)
        selm = arena[0:NF, 7, 0:1024].rearrange("p (h t) -> p h t", t=P)
        ucol = arena[:, 7, 1024:1040]
        gts = arena[0:NF, 8, 0:2048].rearrange("p (b t) -> p b t", t=T)
        dbuf = arena[:, 9, 0:1920].rearrange("p (b t) -> p b t", t=384)
        ebuf = arena[:, 10, 0:1024].rearrange("p (b t) -> p b t", t=T)
        silug = arena[:, 8, :].rearrange("p (b m t) -> p b m t", b=2, t=T)
        prod = arena[:, 9, :].rearrange("p (b m t) -> p b m t", b=2, t=T)

        def hid(base):
            return parts_r[base, 3][:, :, :].rearrange("p a n -> p (a n)")[:, 0:NH * T].rearrange(
                "p (f t) -> p f t", t=T)

        def tok(plane):
            return arena[:, plane, :].rearrange("p (g n) -> p g n", g=2)

        FW = [512] * 5 + [256]

        def level_steps(lv):
            steps = [("u", 0), ("u", 1), ("v", 0), ("u", 2), ("v", 1), ("t", 0), ("u", 3), ("v", 2), ("t", 1),
                     ("v", 3), ("t", 2), ("t", 3)]
            return [st for st in steps if lv < LEVELS or st[0] != "t"]

        @block.tensor
        def _(pe):
            n_used, n_hi_used, n_in, n_h = [0], [0], [0], [0]

            def begin(kind, name):
                jobs, n = (acc_jobs, 2) if kind == "acc" else (aux_jobs, 4)
                a = jobs[name] = len(jobs)
                if a >= n:
                    pe.wait_ge(S(f"{kind}_drained{a % n}"), a // n)
                return (acc if kind == "acc" else aux)[a % n], S(f"{kind}_filled{a % n}"), a // n + 1

            def mm(out, lhsT, rhs, start, stop):
                return pe.matmul(out, lhsT, rhs, start=start, stop=stop, skip_group_check=True)

            def ada_reduce(g):
                ps, filled, _ = begin("aux", f"ada{g}")
                pe.wait_ge(S("ada_summed"), g + 1)
                for m in range(4):
                    last = mm(ps[:, m:m + 1], ada_sum(g)[:, m * P:(m + 1) * P], ones[:, 0:1], m == 0, True)
                last.then_inc(filled, 1)

            def new_input(n=NF):
                base = n_in[0]
                n_in[0] += n
                return lambda k: pe.wait_ge(S("in_ready"), base + k + 1)

            def norm_input():
                base = n_h[0]
                n_h[0] += NF
                return (lambda k: pe.wait_ge(S("h_hi"), base + k + 1)), new_input()

            streamed = []

            def stream(name, w, c0, ncols, nk, x_hi, x_lo, ready=None, tiles=None, srcs=None, reuse=None,
                       before_end=None):
                tiles = tiles or [(m * P, P, m) for m in range(ncols // P)]
                todo = []
                if reuse is not None:
                    todo = [(0, nk, reuse)]
                else:
                    for k0 in range(0, nk, KT if ncols > 256 else 8):
                        n = min(KT if ncols > 256 else 8, nk - k0)
                        src = srcs if srcs else [rows_of(w, k0, n, c0, ncols)]
                        todo.append((k0, n, add_slot("split" if x_lo is not None else "raw", None, src)))
                ps, filled, nth = begin("acc", name)
                after_job[name] = []

                def reduce_ready(before):
                    while 2 * len(streamed) + 1 < len(ada_slots) and ada_slots[2 * len(streamed) + 1] < before:
                        g = len(streamed)
                        streamed.append(g)
                        ada_reduce(g)
                        after_job[name].append(g)

                for k0, n, j in todo:
                    if x_lo is not None:
                        q = len(split_of)
                        split_of.append(j)
                        pe.wait_ge(S("w_hi"), q + 1)
                        w_h, w_l = whi[:, q % 2, :], wlo[:, q % 2, :]
                        if isinstance(ready, tuple):
                            parts = [(w_h, (x_hi,), ready[0]), (w_l, (x_hi,), None), (w_h, (x_lo,), ready[1])]
                        else:
                            parts = [(w_h, (x_hi, x_lo), ready), (w_l, (x_hi,), None)]
                    else:
                        landed(pe, j)
                        parts = [(ring[:, j % RING, :], (x_hi,), ready)]
                    for i, (wt, xs, wait) in enumerate(parts):
                        if i == 1:
                            if len(parts) == 2:
                                n_hi_used[0] += 1
                                last.then_inc(S("w_hi_used"), 1)
                                hi_used.append((S("w_hi_used"), n_hi_used[0]))
                            reduce_ready(j)
                            if before_end and k0 + n == nk:
                                before_end()
                            pe.wait_ge(S("w_split"), q + 1)
                        for i_m, (off, wd, m) in enumerate(tiles):
                            for k in range(n):
                                if wait and i_m == 0:
                                    wait(k0 + k)
                                rows = P if not srcs or k < len(srcs) - 1 else srcs[-1][0]
                                for x in xs:
                                    o = k * ncols + off
                                    last = mm(ps[0:wd, m * T:(m + 1) * T], wt[0:rows, o:o + wd],
                                              x[0:rows, k0 + k, :],
                                              k0 + k == 0 and i == 0 and x is xs[0] and m % 2 == 0,
                                              k0 + k == nk - 1 and i == len(parts) - 1)
                    if k0 + n < nk:
                        n_used[0] += 1
                        last.then_inc(S("w_used"), 1)
                        end = (S("w_used"), n_used[0])
                    else:
                        last.then_inc(filled, 1)
                        end = (filled, nth)
                    if x_lo is not None and len(parts) == 3:
                        hi_used.append(end)
                    if x_lo is not None:
                        used.append(end)
                    else:
                        freed[j] = end
                job_last[name] = max(j for _, _, j in todo)
                reduce_ready(job_last[name])
                if reuse is None:
                    ada_half()
                return todo[-1][2]

            def norm(i, fs=range(NF)):
                if fs[0] == 0:
                    norm_ps[0] = begin("aux", f"norm{i}")[0:2]
                ps, filled = norm_ps[0]
                for f in fs:
                    pe.wait_ge(S("sq_ready"), NF * i + f + 1)
                    last = mm(ps[:, 0:T], ones, pl(14)[:, f, :], f == 0, f == NF - 1)
                if fs[-1] == NF - 1:
                    last.then_inc(filled, 1)

            norm_ps = [None]
            first_half, second_half = range(NF // 2), range(NF // 2, NF)

            def sums(name, sem, lhsT, plane, j):
                ps, filled, _ = begin("aux", f"{name}{j}")
                pe.wait_ge(S(sem), j + 1)
                mm(ps[:, :], lhsT, arena[:, plane, 512 * j:512 * (j + 1)], True, True).then_inc(filled, 1)

            def to_tokens(name, plane, g, b, waits):
                ps, filled, _ = begin("aux", f"{name}{g}{b}")
                waits()
                for m in range(4):
                    last = pe.matmul(ps[:, m * P:(m + 1) * P], pl(plane)[:, 4 * b + m, g * P:(g + 1) * P], ident,
                                     is_transpose=True, start=m == 0, stop=True, skip_group_check=True)
                last.then_inc(filled, 1)

            def ffn(l, wg, cg, wu, cu, wd, next_norm):
                x = (plr(0), plr(1))
                r = norm_input()
                for c, n in enumerate(FW):
                    stream(f"fg{l}{c}", wg, cg + COLS * c, n, NF, *x, ready=r if c == 0 else None)
                    stream(f"fu{l}{c}", wu, cu + COLS * c, n, NF, *x)
                r = new_input(NH)
                for c in range(2):
                    stream(f"fd{l}{c}", wd, COLS * c, COLS, NH, hid(HID_HI), hid(HID_LO), ready=r if c == 0 else None,
                           before_end=(lambda: norm(next_norm, first_half)) if c == 1 else None)
                norm(next_norm, second_half)

            def pair(name, w, c0, planes, ready=None, next_norm=None):
                for c in range(2):
                    stream(f"{name}{c}", w, c0 + COLS * c, COLS, NF, plr(planes[0]), plr(planes[1]),
                           ready=ready if c == 0 else None,
                           before_end=(lambda: norm(next_norm, first_half)) if next_norm and c == 1 else None)
                if next_norm:
                    norm(next_norm, second_half)

            for half in range(2 * N_FIRST):
                ada_half()
            pe.wait_ge(S("cst_in"), 16)
            for g in range(N_FIRST):
                if g == N_FIRST - 2:
                    norm(0)
                streamed.append(g)
                ada_reduce(g)
            w_in = d["w_in"][0]
            pair("q", w_in, 0, A_IN, norm_input())
            pe.wait_ge(S("cst_in"), 32)
            pair("k", w_in, D, A_IN)
            pair("v", w_in, 2 * D, A_IN)
            pair("g", w_in, 3 * D, A_IN)
            for g in range(2):
                for b in range(2):
                    to_tokens("vt", 4, g, b, lambda: wait_drained(pe, "acc", f"v{b}"))
            pair("b", w_in, 4 * D, A_IN)

            def ret_scores(h):
                ps, filled, _ = begin("aux", f"rs{h}")
                pe.wait_ge(S("roped"), 2)
                mm(ps[:, 0:T], pl(3)[:, h, 0:P], pl(2)[:, h, :], True, True)
                mm(ps[:, T:T + P], pl(3)[:, h, P:T], pl(2)[:, h, P:T], False, True).then_inc(filled, 1)

            def weighted(name, h, w, vplane, sem, n, den):
                ps, filled, _ = begin("aux", f"{name}{h}")
                pe.wait_ge(S(sem), n)
                last = mm(ps[:, 0:T], tok(vplane)[:, 0, h * P:(h + 1) * P], w[:, 0:T], True, False)
                last = mm(ps[:, P:T], tok(vplane)[:, 1, h * P:(h + 1) * P], w[:, T:T + P], False, True)
                if den:
                    last = mm(ps[:, T:2 * T], ones, w[:, 0:T], False, False)
                    last = mm(ps[:, T + P:2 * T], ones, w[:, T:T + P], False, True)
                last.then_inc(filled, 1)

            def ret_y(h):
                if h == 0:
                    for g in range(2):
                        for b in range(2):
                            wait_drained(pe, "aux", f"vt{g}{b}")
                weighted("ry", h, pbuf[:, h % 2, :], 5, "ret_w", h + 1, False)

            ret_scores(0)
            ret_scores(1)
            for n, (c0, nm) in enumerate([(5, "c"), (6, "u")]):
                for c in range(2):
                    stream(f"{nm}{c}", w_in, c0 * D + COLS * c, COLS, NF, plr(0), plr(1))
                    h = 2 * (2 * n + c)
                    ret_y(h)
                    ret_y(h + 1)
                    if h + 2 < NF:
                        ret_scores(h + 2)
                        ret_scores(h + 3)
            stream("ga0", w_in, 7 * D, COLS, NF, plr(0), plr(1))
            for h in range(NF):
                wait_drained(pe, "aux", f"ry{h}")
            for j in range(4):
                sums("rmean", "ry_all", ones, 13, j)
            stream("ga1", w_in, 7 * D + COLS, COLS, NF, plr(0), plr(1))
            for j in range(4):
                sums("rvar", "ret_sq", ones, 14, j)
            pair("gb", w_in, 8 * D, A_IN)
            pair("co", d["conv_w_out"][0], 0, B_IN, new_input())
            pair("ro", d["ret_w_out"][0], 0, A_IN, new_input())
            pair("mo", d["mix_w_out"][0], 0, B_IN, new_input(), 1)
            ffn(0, d["ffn_w_gate"][0], 0, d["ffn_w_up"][0], 0, d["ffn_w_down"][0], 2)

            norm(3)
            w_in = d["rw_w_in_2"][0]

            def small(name, w, c0, ncols, x, ready, tiles):
                stream(name, w, c0, ncols, NF, x, None, ready=ready, tiles=tiles)

            small("wl", w_in, D, 64, pl(0), new_input(), [(0, 64, 0)])
            small("al", w_in, 3 * D + 64, 64, pl(1), new_input(), [(0, 64, 0)])
            four = lambda c: [(c * COLS + m * P, P, m) for m in range(4)]
            for nm, src, w, x in (("w2", "wl", d["rw_w2_2"][0], lora[:, 0:1, :]),
                                  ("a2", "al", d["rw_a2_2"][0], lora[:, 1:2, :]),
                                  ("g2", "gl", d["rw_g2_2"][0], lora[:, 2:4, :])):
                if nm == "g2":
                    pair("r", w_in, 0, (0, 1), new_input())
                    pair("kk", w_in, D + 64, (4, 5), new_input())
                    small("gl", w_in, 3 * D + 128, 160, pl(14), new_input(), [(0, P, 0), (P, 32, 1)])
                    for j in range(4):
                        sums("kkn", "kk_sq", blk, 3, j)
                wait_drained(pe, "acc", src)
                if nm == "g2":
                    srcs = [(P, 0, 1, D, w[0:P, :].rearrange("(k p) n -> p k n", k=1)),
                            (32, D, 1, D, w[P:P + 32, :].rearrange("(k p) n -> p k n", k=1))]
                    nk = 2
                else:
                    srcs = [(64, 0, 1, D, w.rearrange("(k p) n -> p k n", k=1))]
                    nk = 1
                j = stream(nm + "0", w, 0, D, nk, x, None, tiles=four(0), srcs=srcs)
                stream(nm + "1", w, 0, D, nk, x, None, tiles=four(1), srcs=srcs, reuse=j)
            for j in range(4):
                sums("bon", "rk_ready", blk, 11, j)
            pair("vv", w_in, 2 * D + 64, (0, 1), new_input())
            for g in range(2):
                for b in range(2):
                    to_tokens("wt", 11, g, b, lambda: wait_drained(pe, "acc", f"vv{b}"))
            rows = [slice(0, 64), slice(64, 128)]
            bh, kh = pl(7), pl(10)
            for g in range(2):
                gs = slice(g * P, (g + 1) * P)
                for h in range(16):
                    f, i = h // 2, h % 2
                    ps, filled, _ = begin("aux", f"m{g}{h}")
                    if h == 0 and g == 0:
                        pe.wait_ge(S("hats"), 8)
                    mm(ps[:, 0:T], bh[rows[i], f, gs], AR[rows[i], f, g, :, :], True, True)
                    mm(ps[:, T:2 * T], kh[rows[i], f, gs], AR[rows[i], f, g, :, :], False, True).then_inc(filled, 1)
                for b in range(4):
                    ps, filled, _ = begin("aux", f"t{g}{b}")
                    pe.wait_ge(S("tt_ready"), (LEVELS + 1) * 4 * g + b + 1)
                    for m in range(4):
                        last = pe.matmul(ps[:, m * P:(m + 1) * P], TT[:, 4 * b + m, :], ident, is_transpose=True,
                                         start=m == 0, stop=True, skip_group_check=True)
                    last.then_inc(filled, 1)
                for nm, src in (("bt", 7), ("kt", 10)):
                    for b in range(2):
                        to_tokens(nm, src, g, b, lambda: None)
                for lv in range(1, LEVELS + 1):
                    for kind, b in level_steps(lv):
                        n = (LEVELS * g + lv - 1) * 4 + b
                        ps, filled, _ = begin("aux", f"{kind}{g}{lv}{b}")
                        if kind == "u":
                            pe.wait_ge(S("nm_ready"), n + 1)
                            wait_drained(pe, "aux", f"t{g}{b}" if lv == 1 else f"t{g}{lv - 1}{b}")
                        else:
                            wait_drained(pe, "aux", f"{'u' if kind == 'v' else 'v'}{g}{lv}{b}")
                        for m in range(4):
                            o = ps[:, m * P:(m + 1) * P]
                            if kind == "u":
                                last = mm(o, NM[:, n % 2, m * P:(m + 1) * P], TI[:, 4 * b + m, :], m == 0, True)
                            elif kind == "v":
                                last = mm(o, UU[:, n % 2, m * P:(m + 1) * P], TT[:, 4 * b + m, :], m == 0, True)
                            else:
                                last = pe.matmul(o, TT[:, 4 * b + m, :], ident, is_transpose=True, start=m == 0,
                                                 stop=True, skip_group_check=True)
                        last.then_inc(filled, 1)
                yps, yfilled, _ = begin("acc", f"y{g}")
                for c in range(2):
                    cs = slice(64 * c, 64 * c + 64)
                    n = 2 * g + c
                    pe.wait_ge(S("state_ready"), 4 * n + 1)
                    for f in range(NF):
                        mm(yps[:, f * P + 64 * c:f * P + 64 * c + 64], state[:, f, :], AR[:, f, g, 1, cs],
                           f % 4 == 0 and c == 0, False)
                    for b in range(2):
                        ps, filled, _ = begin("aux", f"x{n}{b}")
                        if b == 0 and c == 0:
                            for bb in range(4):
                                wait_drained(pe, "aux", f"v{g}{LEVELS}{bb}")
                            for bb in range(2):
                                wait_drained(pe, "aux", f"wt{g}{bb}")
                        for m in range(4):
                            f = 4 * b + m
                            mm(ps[cs, m * P:(m + 1) * P], AR[:, f, g, 0, cs], state[:, f, :], m == 0, False)
                            for i in range(2):
                                o = m * P + 64 * i
                                last = mm(ps[cs, o:o + 64], MM[:, 2 * f + i, T + 64 * c:T + 64 * c + 64],
                                          tok(0)[:, g, f * P + 64 * i:f * P + 64 * i + 64], False, True)
                        last.then_inc(filled, 1)
                    for b in range(2):
                        ps, filled, _ = begin("aux", f"sa{n}{b}")
                        wait_drained(pe, "aux", f"x{n}{b}")
                        for m in range(8):
                            h = 8 * b + m
                            last = mm(ps[cs, 64 * m:64 * m + 64], TT[cs, h, cs], XSA[cs, 64 * h:64 * h + 64],
                                      m == 0, True)
                        last.then_inc(filled, 1)
                    for b in range(2):
                        ps, filled, _ = begin("aux", f"st{n}{b}")
                        wait_drained(pe, "aux", f"sa{n}{b}")
                        if b == 0 and c == 0:
                            for bb in range(2):
                                wait_drained(pe, "aux", f"bt{g}{bb}")
                                wait_drained(pe, "aux", f"kt{g}{bb}")
                        for m in range(4):
                            f = 4 * b + m
                            fs = slice(f * P, (f + 1) * P)
                            mm(ps[:, m * P:(m + 1) * P], BTOK[cs, fs], SAT[cs, fs], m == 0, False)
                            last = mm(ps[:, m * P:(m + 1) * P], KTOK[cs, fs], tok(0)[cs, g, fs], False, True)
                        last.then_inc(filled, 1)
                for h in range(16):
                    f, i = h // 2, h % 2
                    o = yps[rows[i], f * P:(f + 1) * P]
                    mm(o, SAT[:, 64 * h:64 * h + 64], MM[:, h, P:2 * P], False, False)
                    last = mm(o, tok(0)[:, g, 64 * h:64 * h + 64], MM[:, h, 3 * P:4 * P], False, True)
                last.then_inc(yfilled, 1)
            wait_drained(pe, "acc", "y1")
            for j in range(4):
                sums("wmean", "wy_all", blk, 7, j)
            for j in range(4):
                sums("wvar", "rw_sq", blk, 9, j)
            pair("wo", d["rw_w_out_2"][0], 0, (4, 5), new_input(), 4)
            gu = d["ffn_w_gu_2"]
            ffn(1, gu[0], 0, gu[0], FFN, d["ffn_w_down_2"][0], 5)

            w_in = d["ml_w_in_2"][0]
            pair("qk", w_in, 0, A_IN, norm_input())
            pe.wait_ge(S("h_whole"), 2 * NF)
            stream("gt", w_in, 3 * D, 16, NF, pl(8), None, tiles=[(0, NF, 0), (NF, NF, 1)])
            pair("mv", w_in, D, A_IN)
            pair("o", w_in, 2 * D, A_IN)
            ps, filled, _ = begin("aux", "ut")
            pe.wait_ge(S("gates"), 2)
            for g in range(2):
                last = pe.matmul(ps[:, NF * g:NF * (g + 1)], gts[:, 3, g * P:(g + 1) * P], cst[0:NF, C_ID:C_ID + NF],
                                 is_transpose=True, start=g == 0, stop=True, skip_group_check=True)
            last.then_inc(filled, 1)
            for g in range(2):
                for b in range(2):
                    to_tokens("mt", 4, g, b, lambda: wait_drained(pe, "acc", f"mv{b}"))

            def ml_num(h):
                if h == 0:
                    for g in range(2):
                        for b in range(2):
                            wait_drained(pe, "aux", f"mt{g}{b}")
                weighted("nd", h, dbuf[:, 3 + h % 2, :], 6, "ml_w", h + 1, True)

            for h in range(NF):
                ps, filled, _ = begin("aux", f"gb{h}")
                mm(ps[:, :], selm[:, h, :], gts[:, 4:6, :].rearrange("p a t -> p (a t)"), True, True)\
                    .then_inc(filled, 1)
                ps, filled, _ = begin("aux", f"ms{h}")
                pe.wait_ge(S("ml_act"), NF)
                rr = rows[h % 2]
                q, k = pl(3)[rr, h // 2, :], pl(3)[rr, 4 + h // 2, :]
                mm(ps[:, 0:T], k[:, 0:P], q, True, True)
                mm(ps[:, T:T + P], k[:, P:T], q[:, P:T], False, True).then_inc(filled, 1)
                if h >= 1:
                    ml_num(h - 1)
            ml_num(NF - 1)
            for j in range(4):
                sums("msq", "ml_sq", ones, 12, j)
            pair("lo", d["ml_w_out_2"][0], 0, A_IN, new_input(), 6)
            ffn(2, gu[1], 0, gu[1], FFN, d["ffn_w_down_2"][1], 7)

        @block.scalar
        def _(act):
            count = {}

            def do(ins, sig="act_step"):
                count[sig] = count.get(sig, 0) + 1
                last[0] = sig
                ins.then_inc(S(sig), 1)

            last = [None]

            def fence(sig=None):
                act.wait_ge(S(sig or last[0]), count[sig or last[0]])

            f_ = act.activation
            split_at = [0]

            def pump(upto):
                while split_at[0] < len(split_of) and split_of[split_at[0]] <= upto:
                    q = split_at[0]
                    j = split_of[q]
                    _, _, srcs = slots[j]
                    n = sum(s[2] * s[3] for s in srcs)
                    landed(act, j)
                    if q >= 2:
                        act.wait_ge(*hi_used[q - 2])
                        act.wait_ge(S("w_split"), q - 1)
                    f_(whi[:, q % 2, 0:n], ring[:, j % RING, 0:n], ACT.Copy).then_inc(S("w_hi"), 1)
                    split_at[0] += 1

            def job(name):
                pump(ahead(name, 2))

            def drain(kind, name, out, in_, func, last=True, **kw):
                ins = f_(out, in_, func, **kw)
                if last:
                    ins.then_inc(drained(kind, name), 1)
                else:
                    do(ins)

            def drain4(name, plane, c, func):
                job(name)
                ps = wait_filled(act, "acc", name)
                drain("acc", name, arena[:, plane, 1024 * c:1024 * (c + 1)], ps[:, :], func)

            def squares(i, fs):
                if fs[0] == NF // 2 or len(fs) == NF:
                    load_table(ACT.Sqrt)
                for f in fs:
                    if i:
                        act.wait_ge(S("x_ready"), NF * (i - 1) + f + 1)
                    do(f_(pl(14)[:, f, :], X[:, f, :], ACT.Square), "sq_ready")

            def last_pair(name, i):
                job(f"{name}0")
                squares(i, range(NF // 2))
                job(f"{name}1")
                squares(i, range(NF // 2, NF))

            def norm(i):
                ps = wait_filled(act, "aux", f"norm{i}")
                drain("aux", f"norm{i}", rs[:, :], ps[:, 0:T], ACT.Sqrt, scale=1.0 / D, bias=EPS)

            scaled = [0]

            def shift(l, which, val, planes, sig="h_hi"):
                for f in range(NF):
                    act.wait_ge(S("h_scaled"), NF * scaled[0] + f + 1)
                    out = plr(planes[0])[:, f, :] if planes else pl(val)[:, f, :]
                    do(f_(out, pl(val)[:, f, :], ACT.Identity,
                          bias=mods[:, l, 24 * which + f:24 * which + f + 1]), sig)
                scaled[0] += 1

            def load_table(func):
                do(f_(tiny[:, :], cst[:, C_ONE:C_ONE + 1], func))

            def head_inverse(name, plane, scale, eps):
                for j in range(4):
                    ps = wait_filled(act, "aux", f"{name}{j}")
                    drain("aux", f"{name}{j}", arena[:, plane, 512 * j:512 * (j + 1)], ps[:, :], ACT.Ln,
                          scale=scale, bias=eps)
                for j in range(4):
                    act.wait_ge(drained("aux", f"{name}{j}"), aux_jobs[f"{name}{j}"] // 4 + 1)
                    quarter = arena[:, plane, 512 * j:512 * (j + 1)]
                    do(f_(quarter, quarter, ACT.Exp, scale=-0.5), "head_inv")

            def ffn(l, i):
                for c, n in enumerate(FW):
                    job(f"fg{l}{c}")
                    ps = wait_filled(act, "acc", f"fg{l}{c}")
                    if c >= 2:
                        act.wait_ge(S("prod_ready"), len(FW) * l + c - 1)
                    drain("acc", f"fg{l}{c}", silug[:, c % 2, 0:n // P, :].rearrange("p m t -> p (m t)"),
                          ps[:, 0:2 * n], ACT.Silu)
                    job(f"fu{l}{c}")
                last_pair(f"fd{l}", i)

            act.dma_start(posi, d["positions"].partition_broadcast(P)).then_inc(S("pos_in"), 16)
            act.wait_ge(S("vec_in"), 16)
            do(f_(silu_c[:, :], vec[:, 0:16], ACT.Silu), "c_ready")
            act.wait_ge(S("cst_in"), 16)
            act.wait_ge(S("x_in"), 16)
            squares(0, range(NF))
            norm(0)
            shift(0, 0, 13, A_IN)
            pump(9)
            act.wait_ge(S("angles"), 2)
            do(f_(sinb, sinb, ACT.Sin), "trig")
            do(f_(cosb, cosb, ACT.Sin), "trig")
            act.dma_start(arena[:, 11:13, :].rearrange("p a n -> p (a n)")[:, 0:NF * 384], d["dec"])\
                .then_inc(S("dec_in"), 16)
            for nm, plane, func in (("q", 2, ACT.Copy), ("k", 3, ACT.Copy), ("v", 4, ACT.Copy), ("g", 6, ACT.Silu),
                                    ("b", 7, ACT.Copy)):
                for c in range(2):
                    drain4(f"{nm}{c}", plane, c, func)
            def tokens(name, g, b, dst):
                ps = wait_filled(act, "aux", f"{name}{g}{b}")
                drain("aux", f"{name}{g}{b}", dst[:, 512 * b:512 * (b + 1)], ps[:, :], ACT.Copy)

            def ret_drain(h):
                ps = wait_filled(act, "aux", f"ry{h}")
                drain("aux", f"ry{h}", pl(13)[:, h, :], ps[:, 0:T], ACT.Copy)

            for n in range(4):
                if n < 2:
                    drain4(f"c{n}", 8, n, ACT.Copy)
                else:
                    job(f"u{n - 2}")
                ret_drain(2 * n)
                ret_drain(2 * n + 1)
            drain4("ga0", 9, 0, ACT.Sigmoid)
            for j in range(4):
                act.wait_ge(S("ret_c"), j + 1)
                do(f_(arena[:, 14, 512 * j:512 * (j + 1)], arena[:, 13, 512 * j:512 * (j + 1)], ACT.Square), "ret_sq")
            drain4("ga1", 9, 1, ACT.Sigmoid)
            load_table(ACT.Ln)
            head_inverse("rvar", 14, 1.0 / P, EPS)
            drain4("gb0", 10, 0, ACT.Sigmoid)
            drain4("gb1", 10, 1, ACT.Sigmoid)
            for nm in ("co", "ro"):
                for c in range(2):
                    job(f"{nm}{c}")
            last_pair("mo", 1)
            norm(1)
            shift(0, 1, 13, A_IN)
            ffn(0, 2)
            norm(2)
            squares(3, range(NF))
            norm(3)
            shift(1, 0, 2, None, "h_whole")

            for nm, rws, b, func in (("wl", 64, 0, ACT.Tanh), ("al", 64, 1, ACT.Copy)):
                job(nm)
                ps = wait_filled(act, "acc", nm)
                drain("acc", nm, lora[0:rws, b, :], ps[0:rws, 0:T], func)
            for nm, bias, plane in (("w2", "rw_w0_2", 6), ("a2", "rw_a0_2", 7)):
                for c in range(2):
                    job(f"{nm}{c}")
                    ps = wait_filled(act, "acc", f"{nm}{c}")
                    for m in range(4):
                        drain("acc", f"{nm}{c}", pl(plane)[:, 4 * c + m, :], ps[:, m * T:(m + 1) * T], ACT.Sigmoid,
                              last=m == 3, bias=V(bias, 4 * c + m))
            for nm, plane in (("r", 9), ("kk", 10)):
                for c in range(2):
                    drain4(f"{nm}{c}", plane, c, ACT.Copy)
            for j in range(4):
                act.wait_ge(S("kk_raw"), 2 * j + 2)
                do(f_(arena[:, 3, 512 * j:512 * (j + 1)], arena[:, 2, 512 * j:512 * (j + 1)], ACT.Square), "kk_sq")
            job("gl")
            ps = wait_filled(act, "acc", "gl")
            do(f_(lora[:, 2, :], ps[:, 0:T], ACT.Sigmoid))
            drain("acc", "gl", lora[0:32, 3, :], ps[0:32, T:2 * T], ACT.Sigmoid)
            act.wait_ge(S("cum_ready"), 1)
            do(f_(arena[:, 14, :], arena[:, 12, :], ACT.Exp, scale=-KAPPA), "decays")
            do(f_(arena[:, 13, :], arena[:, 12, :], ACT.Exp, scale=KAPPA), "decays")
            load_table(ACT.Ln)
            for j in range(4):
                act.wait_ge(S("kk_sums"), j + 1)
                quarter = arena[:, 3, 512 * j:512 * (j + 1)]
                do(f_(quarter, quarter, ACT.Ln))
            for j in range(4):
                fence()
                quarter = arena[:, 3, 512 * j:512 * (j + 1)]
                do(f_(quarter, quarter, ACT.Exp, scale=-0.5), "head_inv")
            for c in range(2):
                drain4(f"g2{c}", 8, c, ACT.Copy)
            for j in range(4):
                ps = wait_filled(act, "aux", f"bon{j}")
                drain("aux", f"bon{j}", arena[:, 6, 512 * j:512 * (j + 1)], ps[:, :], ACT.Copy)
            for c in range(2):
                drain4(f"vv{c}", 11, c, ACT.Copy)
            for g in range(2):
                for b in range(2):
                    tokens("wt", g, b, tok(0)[:, g, :])

            def turn(name, g, b):
                ps = wait_filled(act, "aux", name)
                drain("aux", name, TI[:, 4 * b:4 * b + 4, :].rearrange("p h t -> p (h t)"), ps[:, :], ACT.Copy)

            for g in range(2):
                for b in range(4):
                    turn(f"t{g}{b}", g, b)
                for nm, dst in (("bt", BTOK), ("kt", KTOK)):
                    for b in range(2):
                        tokens(nm, g, b, dst)
                for lv in range(1, LEVELS + 1):
                    for kind, b in level_steps(lv):
                        n = (LEVELS * g + lv - 1) * 4 + b
                        if kind == "u":
                            ps = wait_filled(act, "aux", f"u{g}{lv}{b}")
                            drain("aux", f"u{g}{lv}{b}", UU[:, n % 2, :], ps[:, :], ACT.Copy)
                        elif kind == "t":
                            turn(f"t{g}{lv}{b}", g, b)
                for c in range(2):
                    cs = slice(64 * c, 64 * c + 64)
                    n = 2 * g + c
                    for b in range(2):
                        ps = wait_filled(act, "aux", f"x{n}{b}")
                        drain("aux", f"x{n}{b}", XSA[cs, 512 * b:512 * (b + 1)], ps[cs, :], ACT.Copy)
                ps = wait_filled(act, "acc", f"y{g}")
                drain("acc", f"y{g}", pl(7)[:, :, g * P:(g + 1) * P], ps[:, :].rearrange("p (f t) -> p f t", t=P), ACT.Copy)
            for j in range(4):
                act.wait_ge(S("rw_c"), j + 1)
                do(f_(arena[:, 9, 512 * j:512 * (j + 1)], arena[:, 7, 512 * j:512 * (j + 1)], ACT.Square), "rw_sq")
            load_table(ACT.Ln)
            head_inverse("wvar", 9, 1.0 / 64, GN_EPS)
            last_pair("wo", 4)
            norm(4)
            shift(1, 1, 13, A_IN)
            ffn(1, 5)

            norm(5)
            shift(2, 0, 13, A_IN)
            for f in range(NF):
                do(f_(pl(8)[:, f, :], pl(13)[:, f, :], ACT.Identity, bias=mods[:, 2, f:f + 1]), "h_whole")
            act.dma_start(selm, d["sel"].rearrange("k (h t) -> k h t", t=P)).then_inc(S("sel"), 16)
            act.dma_start(gateb[:, 0:1], d["ml_b_i_2"].rearrange("a h -> h a")).then_inc(S("sel"), 16)
            act.dma_start(gateb[:, 1:2], d["ml_b_f_2"].rearrange("a h -> h a")).then_inc(S("sel"), 16)
            for c in range(2):
                drain4(f"qk{c}", 2, c, ACT.Copy)
            job("gt")
            act.wait_ge(S("gate_b"), 1)
            ps = wait_filled(act, "acc", "gt")
            do(f_(gts[:, 0, :], ps[0:NF, 0:T], ACT.Tanh, scale=1.0 / CAP, bias=gateb[:, 0:1]))
            drain("acc", "gt", gts[:, 1, :], ps[0:NF, T:2 * T], ACT.Tanh, scale=1.0 / CAP, bias=gateb[:, 1:2])
            act.wait_ge(drained("acc", "gt"), acc_jobs["gt"] // 2 + 1)
            do(f_(gts[:, 1, :], gts[:, 1, :], ACT.Exp, scale=-CAP))
            fence()
            do(f_(gts[:, 1, :], gts[:, 1, :], ACT.Ln, bias=1.0), "softplus")
            for nm, plane, func in (("mv", 4, ACT.Copy), ("o", 5, ACT.Sigmoid)):
                for c in range(2):
                    drain4(f"{nm}{c}", plane, c, func)
            for f in range(NF):
                act.wait_ge(S("ml_conv"), f + 1)
                do(f_(pl(3)[:, f, :], pl(12)[:, f, :], ACT.Silu), "ml_act")
            for g in range(2):
                for b in range(2):
                    tokens("mt", g, b, tok(6)[:, g, :])
            for h in range(NF):
                ps = wait_filled(act, "aux", f"gb{h}")
                act.wait_ge(S("ml_dd"), 2 * h + 2)
                do(f_(dbuf[:, h % 2, :], dbuf[:, h % 2, :], ACT.Exp, scale=-1.0), "ml_de")
                if h >= 2:
                    act.wait_ge(S("ml_y"), h - 1)
                drain("aux", f"gb{h}", ebuf[:, h % 2, :], ps[:, T:2 * T], ACT.Exp)
            for j in range(4):
                act.wait_ge(S("ml_y"), 2 * j + 2)
                do(f_(arena[:, 12, 512 * j:512 * (j + 1)], arena[:, 11, 512 * j:512 * (j + 1)], ACT.Square), "ml_sq")
            load_table(ACT.Ln)
            head_inverse("msq", 12, 1.0 / P, EPS)
            last_pair("lo", 6)
            norm(6)
            shift(2, 1, 13, A_IN)
            ffn(2, 7)
            norm(7)

        @block.gpsimd
        def _(pool):
            for g in range(2):
                for lv in range(1, LEVELS + 1):
                    for b in range(4):
                        n = (LEVELS * g + lv - 1) * 4 + b
                        if lv == 1:
                            pool.wait_ge(S("mm_ready"), 16 * g + 4 * b + 4)
                        if n >= 2:
                            m = n - 2
                            wait_filled(pool, "aux", f"u{m // (4 * LEVELS)}{m // 4 % LEVELS + 1}{m % 4}")
                        pool.tensor_tensor(NM[:, n % 2, :].rearrange("p (h t) -> p h t", t=P),
                                           MM[:, 4 * b:4 * b + 4, 0:P],
                                           bcast(cc(C_LVL + lv * P), 4), ALU.mult)\
                            .then_inc(S("nm_ready"), 1)
            for h in range(NF):
                pool.wait_ge(S("ml_de"), h + 1)
                diag = dbuf[:, h % 2, :].rearrange("p (b t) -> p b t", t=P)[:, 0:3:2, :]
                pool.tensor_tensor(diag, diag, bcast(cc(C_CAUS), 2), ALU.mult).then_inc(S("ml_mask"), 1)

        @block.vector
        def _(dve):
            count = {}

            def do(ins, sig="dve_step"):
                count[sig] = count.get(sig, 0) + 1
                last[0] = sig
                ins.then_inc(S(sig), 1)
                return count[sig]

            last = [None]

            def fence(sig=None):
                dve.wait_ge(S(sig or last[0]), count[sig or last[0]])

            tt, ts, stt = dve.tensor_tensor, dve.tensor_scalar, dve.scalar_tensor_tensor
            cp = dve.tensor_copy
            at = [0]
            n_split, n_ada = [0], [0]

            def pump(upto):
                while at[0] <= min(upto, len(slots) - 1):
                    j = at[0]
                    kind, _, srcs = slots[j]
                    if kind == "split":
                        q = n_split[0]
                        n = sum(s[2] * s[3] for s in srcs)
                        dve.wait_ge(S("w_hi"), q + 1)
                        if q >= 2:
                            dve.wait_ge(*used[q - 2])
                        tt(wlo[:, q % 2, 0:n], ring[:, j % RING, 0:n], whi[:, q % 2, 0:n].bitcast(F32),
                           ALU.subtract).then_inc(S("w_split"), 1)
                        freed[j] = (S("w_split"), q + 1)
                        n_split[0] += 1
                    elif kind == "ada":
                        g, half = n_ada[0] // 2, n_ada[0] % 2
                        cs = silu_c[:, (0 if g < 12 else 8) + KT * half:][:, 0:KT]
                        if g == 0 and half == 0:
                            dve.wait_ge(S("c_ready"), 1)
                        landed(dve, j)
                        if half == 0 and g > N_FIRST:
                            wait_filled(dve, "aux", f"ada{g - 1}")
                        for k in range(KT):
                            w = ring[:, j % RING, k * COLS:(k + 1) * COLS]
                            if half == 0 and k == 0:
                                last_ada[0] = (S("dve_step"), do(ts(ada_sum(g), w, cs[:, 0:1], None, ALU.mult)))
                                continue
                            dve.wait_ge(*last_ada[0])
                            sig = "dve_step" if k < KT - 1 else ("ada_half", "ada_summed")[half]
                            n = do(stt(out=ada_sum(g), in0=w, scalar=cs[:, k:k + 1], in1=ada_sum(g),
                                       op0=ALU.mult, op1=ALU.add), sig)
                            last_ada[0] = (S(sig), n)
                        freed[j] = last_ada[0]
                        n_ada[0] += 1
                    at[0] += 1

            last_ada = [None]

            def ada_finish(g):
                ps = wait_filled(dve, "aux", f"ada{g}")
                l, c = g // 12, 4 * (g % 12)
                b = V("ada_b", c, 4) if l == 0 else V("ada_b_2", 48 * (l - 1) + c, 4)
                tt(mods[:, l, c:c + 4], ps[:, 0:4], b, ALU.add).then_inc(drained("aux", f"ada{g}"), 1)
                ada_done[0] = g

            ada_done = [-1]

            def job(name):
                pump(ahead(name, 1))

            def done(name):
                for g in after_job[name]:
                    ada_finish(g)
                pump(ahead(name, 2))

            def mod(l, i, f=0, n=1):
                g = 12 * l + (8 * i + f + n - 1) // 4
                assert g <= ada_done[0], (l, i, g, ada_done[0])
                return mods[:, l, 8 * i + f:8 * i + f + n]

            def mods_ready(l, i):
                g = 12 * l + (8 * i + 7) // 4
                assert g <= ada_done[0]
                wait_drained(dve, "aux", f"ada{g}")

            def to_input(planes, val, f, nhid=None, sig="in_ready"):
                hi, lo = planes
                n = do(cp(hi, val))
                dve.wait_ge(S("dve_step"), n)
                do(tt(lo, val, hi.bitcast(F32), ALU.subtract), sig)

            def plane_input(planes, plane, fs=range(NF)):
                hi, lo, val = plr(planes[0]), plr(planes[1]), pl(plane)
                n = do(cp(hi[:, fs[0], :], val[:, fs[0], :]))
                for f in fs:
                    m = n
                    if f != fs[-1]:
                        n = do(cp(hi[:, f + 1, :], val[:, f + 1, :]))
                    dve.wait_ge(S("dve_step"), m)
                    do(tt(lo[:, f, :], val[:, f, :], hi[:, f, :].bitcast(F32), ALU.subtract), "in_ready")
                fence()

            def norm_scale(i):
                wait_drained(dve, "aux", f"norm{i}")
                do(dve.reciprocal(rs[:, :], rs[:, :]))
                fence()

            def norm_mod(i, l, which, gain, val, planes, sig="in_ready"):
                mods_ready(l, 3 * which + 1)
                sc, sh = mod(l, 3 * which + 1, 0, NF), 3 * which
                if gain:
                    do(stt(out=nscale[:, :], in0=sc, scalar=1.0, in1=V(gain, 0, NF), op0=ALU.add, op1=ALU.mult))
                else:
                    do(ts(nscale[:, :], sc, 1.0, None, ALU.add))
                fence()
                if i > 0:
                    norm_scale(i)
                for f in range(NF):
                    do(stt(out=pl(val)[:, f, :], in0=X[:, f, :], scalar=nscale[:, f:f + 1], in1=rs[:, :],
                           op0=ALU.mult, op1=ALU.mult), "h_scaled")
                if planes:
                    for f in range(NF):
                        dve.wait_ge(S("h_hi"), norm_mods[0] * NF + f + 1)
                        do(stt(out=plr(planes[1])[:, f, :], in0=pl(val)[:, f, :], scalar=mod(l, sh, f),
                               in1=plr(planes[0])[:, f, :].bitcast(F32), op0=ALU.add, op1=ALU.subtract), "in_ready")
                    norm_mods[0] += 1
                pump(later[0])

            norm_mods, later = [0], [-1]

            def head_center(name, plane, n, sig):
                for j in range(4):
                    ps = wait_filled(dve, "aux", f"{name}mean{j}")
                    y = arena[:, plane, 512 * j:512 * (j + 1)]
                    stt(out=y, in0=ps[:, :], scalar=-1.0 / n, in1=y, op0=ALU.mult, op1=ALU.add)\
                        .then_inc(drained("aux", f"{name}mean{j}"), 1)

            n_head_inv = [0]

            def head_inv_ready():
                n_head_inv[0] += 1
                dve.wait_ge(S("head_inv"), n_head_inv[0])

            def head_scale(plane, sqp):
                for j in range(4):
                    sl = slice(512 * j, 512 * (j + 1))
                    head_inv_ready()
                    do(tt(arena[:, plane, sl], arena[:, plane, sl], arena[:, sqp, sl], ALU.mult))

            def update_x(name, l, i):
                for c in range(2):
                    job(f"{name}{c}")
                    ps = wait_filled(dve, "acc", f"{name}{c}")
                    for m in range(4):
                        f = 4 * c + m
                        do(stt(out=X[:, f, :], in0=ps[:, m * T:(m + 1) * T], scalar=mod(l, i, f), in1=X[:, f, :],
                               op0=ALU.mult, op1=ALU.add), "x_ready")
                    dve_drained(f"{name}{c}")
                    if c == 0:
                        done(f"{name}{c}")
                for g in after_job[f"{name}1"]:
                    ada_finish(g)
                later[0] = ahead(f"{name}1", 2)

            def dve_drained(name):
                dve.wait_ge(S("x_ready"), count["x_ready"])
                dve.sem_inc(drained("acc", name), 1)

            def ffn(l, ml, mw):
                for c, n in enumerate(FW):
                    job(f"fg{l}{c}")
                    done(f"fg{l}{c}")
                    job(f"fu{l}{c}")
                    wait_drained(dve, "acc", f"fg{l}{c}")
                    ps = wait_filled(dve, "acc", f"fu{l}{c}")
                    pr = prod[:, c % 2, 0:n // P, :]
                    tt(pr.rearrange("p m t -> p (m t)"), ps[:, 0:2 * n],
                       silug[:, c % 2, 0:n // P, :].rearrange("p m t -> p (m t)"), ALU.mult)\
                        .then_inc(drained("acc", f"fu{l}{c}"), 1)
                    wait_drained(dve, "acc", f"fu{l}{c}")
                    o = slice(4 * c, 4 * c + n // P)
                    k = do(cp(hid(HID_HI)[:, o, :], pr), "prod_ready")
                    dve.wait_ge(S("prod_ready"), k)
                    for m in range(n // P):
                        do(tt(hid(HID_LO)[:, 4 * c + m, :], pr[:, m, :],
                              hid(HID_HI)[:, 4 * c + m, :].bitcast(F32), ALU.subtract), "in_ready")
                    done(f"fu{l}{c}")
                update_x(f"fd{l}", ml, mw)

            def skip(names):
                for n in names:
                    job(n)
                    done(n)

            pump(2 * N_FIRST - 3)
            for g in range(N_FIRST - 2):
                ada_finish(g)
            norm_scale(0)
            pump(2 * N_FIRST - 1)
            for g in range(N_FIRST - 2, N_FIRST):
                ada_finish(g)
            norm_mod(0, 0, 0, "norm_mix_g", 13, A_IN)
            pump(9)
            dve.wait_ge(S("pos_in"), 16)
            dve.wait_ge(S("cst_in"), 32)
            scr = pl(9)
            do(cp(scr[:, 0, :], posi))
            fence()
            do(ts(scr[:, 0, :], scr[:, 0, :], cc(C_FREQ, 1), None, ALU.mult))
            fence()
            for dst, quarter in ((sinb, 0.0), (cosb, 0.25)):
                n = scr[:, 1, :]
                do(ts(n, scr[:, 0, :], float(1 / (2 * np.pi)), quarter, ALU.mult, ALU.add))
                fence()
                do(ts(n, n, 12582912.0, None, ALU.add))
                fence()
                do(ts(n, n, 12582912.0, None, ALU.subtract))
                fence()
                src = scr[:, 0, :]
                for part in TWO_PI:
                    do(stt(out=dst, in0=n, scalar=-part, in1=src, op0=ALU.mult, op1=ALU.add))
                    fence()
                    src = dst
                if quarter:
                    do(ts(dst, dst, float(np.pi / 2), None, ALU.add))
                    fence()
                do(ts(dst, dst, 3.1415925, -3.1415925, ALU.min, ALU.max), "angles")
            dve.wait_ge(S("trig"), 2)
            do(ts(sinb, sinb, cc(C_FREQ + 1, 1), None, ALU.mult))
            fence()

            def rope(plane, nm):
                for c in range(2):
                    wait_drained(dve, "acc", f"{nm}{c}")
                t, tmp = pl(plane), pl(14)
                for a, b in ((slice(0, 64), slice(64, 128)), (slice(64, 128), slice(0, 64))):
                    do(tt(tmp[a, :, :], t[b, :, :], bcast(sinb[b, :], NF), ALU.mult))
                fence()
                do(tt(t, t, bcast(cosb, NF), ALU.mult))
                fence()
                do(tt(t, t, tmp, ALU.add), "roped")
                fence("roped")

            skip(["q0", "q1", "k0"])
            rope(2, "q")
            skip(["k1", "v0"])
            rope(3, "k")
            skip(["v1", "g0", "g1"])
            for g in range(2):
                for b in range(2):
                    ps = wait_filled(dve, "aux", f"vt{g}{b}")
                    cp(tok(5)[:, g, 512 * b:512 * (b + 1)], ps[:, :]).then_inc(drained("aux", f"vt{g}{b}"), 1)
            skip(["b0", "b1"])

            def ret_weights(h):
                ps = wait_filled(dve, "aux", f"rs{h}")
                if h >= 2:
                    wait_filled(dve, "aux", f"ry{h - 2}")
                tt(pbuf[:, h % 2, :], ps[:, 0:384], dec[:, h, :], ALU.mult).then_inc(drained("aux", f"rs{h}"), 1)
                wait_drained(dve, "aux", f"rs{h}")
                dve.sem_inc(S("ret_w"), 1)

            dve.wait_ge(S("dec_in"), 16)
            ret_weights(0)
            ret_weights(1)
            for n in range(4):
                nm = f"c{n}" if n < 2 else f"u{n - 2}"
                job(nm)
                if n >= 2:
                    c = n - 2
                    ps = wait_filled(dve, "acc", nm)
                    wait_drained(dve, "acc", f"c{c}")
                    o = arena[:, 8, 1024 * c:1024 * (c + 1)]
                    tt(o, ps[:, :], o, ALU.mult).then_inc(drained("acc", nm), 1)
                done(nm)
                if n < 3:
                    ret_weights(2 * n + 2)
                    ret_weights(2 * n + 3)
            job("ga0")
            done("ga0")
            for h in range(NF):
                wait_drained(dve, "aux", f"ry{h}")
            dve.sem_inc(S("ry_all"), 4)
            head_center("r", 13, P, "ret_c")
            for j in range(4):
                wait_drained(dve, "aux", f"rmean{j}")
                dve.sem_inc(S("ret_c"), 1)
            job("ga1")
            done("ga1")
            for c in range(2):
                wait_drained(dve, "acc", f"u{c}")
                wait_drained(dve, "acc", f"b{c}")
            u, cv = pl(8), pl(5)
            for f in range(NF):
                do(ts(cv[:, f, :], u[:, f, :], V("conv_w", 16 + f), None, ALU.mult))
                fence()
                for tap, back in ((1, 1), (0, 2)):
                    do(stt(out=cv[:, f, back:T], in0=u[:, f, 0:T - back], scalar=V("conv_w", 8 * tap + f),
                           in1=cv[:, f, back:T], op0=ALU.mult, op1=ALU.add))
                    fence()
                do(tt(pl(7)[:, f, :], pl(7)[:, f, :], cv[:, f, :], ALU.mult))
                fence()
                to_input((plr(2)[:, f, :], plr(3)[:, f, :]), pl(7)[:, f, :], f)
                if f == 2:
                    job("gb0")
                if f == 4:
                    done("gb0")
            head_scale(13, 14)
            fence()
            do(tt(arena[:, 6, :], arena[:, 6, :], arena[:, 13, :], ALU.mult))
            fence()
            job("gb1")
            done("gb1")
            wait_filled(dve, "acc", "gb1")
            plane_input(A_IN, 6)
            for c in range(2):
                job(f"co{c}")
                wait_drained(dve, "acc", f"gb{c}")
                ps = wait_filled(dve, "acc", f"co{c}")
                tt(arena[:, 8, 1024 * c:1024 * (c + 1)], ps[:, :], arena[:, 10, 1024 * c:1024 * (c + 1)], ALU.mult)\
                    .then_inc(drained("acc", f"co{c}"), 1)
                done(f"co{c}")
            for c in range(2):
                job(f"ro{c}")
                ps = wait_filled(dve, "acc", f"ro{c}")
                o = arena[:, 9, 1024 * c:1024 * (c + 1)]
                tt(o, ps[:, :], o, ALU.mult).then_inc(drained("acc", f"ro{c}"), 1)
                wait_drained(dve, "acc", f"ro{c}")
                wait_drained(dve, "acc", f"co{c}")
                do(tt(o, o, arena[:, 8, 1024 * c:1024 * (c + 1)], ALU.add))
                fence()
                plane_input(B_IN, 9, range(4 * c, 4 * c + 4))
                done(f"ro{c}")
            update_x("mo", 0, 2)
            norm_mod(1, 0, 1, "norm_ffn_g", 13, A_IN)
            ffn(0, 0, 5)
            norm_scale(2)
            for f in range(NF):
                do(stt(out=X[:, f, :], in0=X[:, f, :], scalar=V("final_norm_g", f), in1=rs[:, :], op0=ALU.mult,
                       op1=ALU.mult), "x_ready")

            norm_mod(3, 1, 0, None, 2, None)
            dve.wait_ge(S("h_whole"), NF)
            hf, xx = pl(2), pl(3)
            do(tt(xx[:, :, 1:T], hf[:, :, 0:T - 1], hf[:, :, 1:T], ALU.subtract))
            do(ts(xx[:, :, 0:1], hf[:, :, 0:1], -1.0, None, ALU.mult))
            fence()

            def mixed(i, plane, sig="in_ready"):
                for f in range(NF):
                    do(stt(out=pl(plane)[:, f, :], in0=xx[:, f, :], scalar=V("rw_mix_2", 8 * i + f), in1=hf[:, f, :],
                           op0=ALU.mult, op1=ALU.add), sig)

            mixed(1, 0)
            mixed(4, 1)
            mixed(0, 13, "dve_step")
            fence()
            skip(["wl", "al"])
            wait_filled(dve, "acc", "al")
            plane_input((0, 1), 13)
            mixed(2, 13, "dve_step")
            fence()
            skip(["w20", "w21"])
            plane_input((4, 5), 13)
            mixed(5, 14)
            mixed(3, 13, "dve_step")
            skip(["a20", "a21"])
            for c in range(2):
                wait_drained(dve, "acc", f"w2{c}")
            ld, cum = pl(6), pl(12)
            for f in range(NF):
                for n in range(4):
                    sl = slice(64 * n, 64 * n + 64)
                    do(dve.tensor_tensor_scan(cum[:, f, sl], ld[:, f, sl], cst[:, C_ZERO:C_ZERO + 64], 0.0,
                                              ALU.add, ALU.add))
                if f == 3:
                    skip(["r0"])
            skip(["r1"])
            wait_filled(dve, "acc", "r1")
            plane_input((0, 1), 13)
            dve.sem_inc(S("cum_ready"), 1)
            skip(["kk0", "kk1"])
            for c in range(2):
                wait_drained(dve, "acc", f"kk{c}")
                wait_drained(dve, "acc", f"a2{c}")
                wait_drained(dve, "acc", f"r{c}")
            for f in range(NF):
                do(ts(pl(2)[:, f, :], pl(10)[:, f, :], V("rw_k_k_2", f), None, ALU.mult), "kk_raw")
            job("gl")
            for f in range(NF):
                do(ts(pl(11)[:, f, :], pl(7)[:, f, :], 1.0, V("rw_k_a_2", f), ALU.subtract, ALU.mult))
            fence()
            do(stt(out=arena[:, 10, :], in0=arena[:, 11, :], scalar=1.0, in1=arena[:, 10, :], op0=ALU.add,
                   op1=ALU.mult))
            fence()
            for f in range(NF):
                do(stt(out=pl(11)[:, f, :], in0=pl(9)[:, f, :], scalar=V("rw_r_k_2", f), in1=pl(10)[:, f, :],
                       op0=ALU.mult, op1=ALU.mult))
            fence()
            dve.sem_inc(S("rk_ready"), 4)
            done("gl")
            for j in range(4):
                ps = wait_filled(dve, "aux", f"kkn{j}")
                ts(arena[:, 3, 512 * j:512 * (j + 1)], ps[:, :], 1e-24, None, ALU.max)\
                    .then_inc(drained("aux", f"kkn{j}"), 1)
                wait_drained(dve, "aux", f"kkn{j}")
                dve.sem_inc(S("kk_sums"), 1)
            dve.wait_ge(S("decays"), 1)
            do(cp(pend[:, :, :], pl(14)[:, :, 63::64]))
            for g in range(2):
                gs = slice(g * P, (g + 1) * P)
                do(tt(AR[:, :, g, 1, :], pl(9)[:, :, gs], pl(14)[:, :, gs], ALU.mult), "hats")
            job("g20")
            dve.wait_ge(S("decays"), 2)
            do(tt(arena[:, 10, :], arena[:, 10, :], arena[:, 13, :], ALU.mult), "hats")
            do(tt(arena[:, 7, :], arena[:, 7, :], arena[:, 13, :], ALU.mult))
            done("g20")
            for j in range(4):
                sl = slice(512 * j, 512 * (j + 1))
                head_inv_ready()
                do(stt(out=arena[:, 2, sl], in0=arena[:, 2, sl], scalar=-1.0, in1=arena[:, 3, sl], op0=ALU.mult,
                       op1=ALU.mult))
                if j == 1:
                    skip(["g21"])
            fence()
            do(stt(out=arena[:, 7, :], in0=arena[:, 7, :], scalar=-1.0, in1=arena[:, 2, :], op0=ALU.mult,
                   op1=ALU.mult), "hats")
            job("vv0")
            for g in range(2):
                a_hat = AR[:, :, g, 0, :]
                kkn, em = pl(2)[:, :, g * P:(g + 1) * P], pl(14)[:, :, g * P:(g + 1) * P]
                do(cp(a_hat[:, :, 0::64], kkn[:, :, 0::64]), "hats")
                for c in range(2):
                    do(tt(a_hat[:, :, 64 * c + 1:64 * c + 64], kkn[:, :, 64 * c + 1:64 * c + 64],
                          em[:, :, 64 * c:64 * c + 63], ALU.mult), "hats" if c else "dve_step")
            done("vv0")
            skip(["vv1"])
            for c in range(2):
                wait_drained(dve, "acc", f"vv{c}")
            wait_drained(dve, "aux", "bon3")
            do(tt(arena[:, 6, :], arena[:, 6, :], arena[:, 11, :], ALU.mult))
            fence()
            fence("hats")
            do(dve.memset(state[:, :, :], 0.0))
            fence()
            dve.sem_inc(S("state_ready"), 4)
            for g in range(2):
                for h in range(16):
                    ps = wait_filled(dve, "aux", f"m{g}{h}")
                    if h == 0:
                        if g == 0:
                            for gg in range(2):
                                for bb in range(2):
                                    wait_drained(dve, "aux", f"wt{gg}{bb}")
                        else:
                            wait_filled(dve, "acc", "y0")
                    tt(MM[:, h, :].rearrange("p (a t) -> p a t", a=2), ps[:, :].rearrange("p (a t) -> p a t", a=2),
                       bcast(cc(C_MASK, 256), 2), ALU.mult).then_inc(drained("aux", f"m{g}{h}"), 1)
                    if h % 4 == 3:
                        b = h // 4
                        wait_drained(dve, "aux", f"m{g}{h}")
                        dve.sem_inc(S("mm_ready"), 4)
                        sl = slice(4 * b, 4 * b + 4)
                        do(tt(TT[:, sl, :], MM[:, sl, 0:P], bcast(cc(C_LVL), 4), ALU.mult))
                        fence()
                        do(tt(TT[:, sl, :], TT[:, sl, :], bcast(ident, 4), ALU.add), "tt_ready")
                for lv in range(1, LEVELS + 1):
                    for b in range(4):
                        sl = slice(4 * b, 4 * b + 4)
                        ps = wait_filled(dve, "aux", f"v{g}{lv}{b}")
                        t = TT[:, sl, :].rearrange("p h t -> p (h t)")
                        if lv == 1:
                            fence("tt_ready")
                        tt(t, ps[:, :], t, ALU.add).then_inc(drained("aux", f"v{g}{lv}{b}"), 1)
                dve.sem_inc(S("tt_ready"), 4 * LEVELS)
                count["tt_ready"] += 4 * LEVELS
                for c in range(2):
                    cs = slice(64 * c, 64 * c + 64)
                    n = 2 * g + c
                    for b in range(2):
                        ps = wait_filled(dve, "aux", f"sa{n}{b}")
                        cp(SAT[cs, 512 * b:512 * (b + 1)], ps[cs, :]).then_inc(drained("aux", f"sa{n}{b}"), 1)
                    for b in range(2):
                        ps = wait_filled(dve, "aux", f"st{n}{b}")
                        for i in range(2):
                            rr = slice(64 * i, 64 * i + 64)
                            s = state[rr, 4 * b:4 * b + 4, 64 * i:64 * i + 64]
                            ins = tt(s, ps[rr, :].rearrange("p (f v) -> p f v", v=P)[:, :, 64 * i:64 * i + 64], s,
                                     ALU.add)
                            if i == 1:
                                ins.then_inc(drained("aux", f"st{n}{b}"), 1)
                                wait_drained(dve, "aux", f"st{n}{b}")
                            else:
                                do(ins)
                        for i in range(2):
                            rr = slice(64 * i, 64 * i + 64)
                            s = state[rr, 4 * b:4 * b + 4, 64 * i:64 * i + 64]
                            do(tt(s, s, pend[rr, 4 * b:4 * b + 4, n:n + 1].to_broadcast([64, 4, 64]), ALU.mult))
                    fence()
                    dve.sem_inc(S("state_ready"), 4)
            wait_drained(dve, "acc", "y1")
            wait_drained(dve, "acc", "y0")
            dve.sem_inc(S("wy_all"), 4)
            head_center("w", 7, 64, "rw_c")
            for j in range(4):
                wait_drained(dve, "aux", f"wmean{j}")
                dve.sem_inc(S("rw_c"), 1)
            head_scale(7, 9)
            fence()
            for f in range(NF):
                y = pl(7)[:, f, :]
                do(ts(y, y, V("rw_gn_w_2", f), V("rw_gn_b_2", f), ALU.mult, ALU.add))
                fence()
                do(tt(y, y, pl(6)[:, f, :], ALU.add))
                fence()
                do(tt(y, y, pl(8)[:, f, :], ALU.mult))
                fence()
                to_input((plr(4)[:, f, :], plr(5)[:, f, :]), y, f)
            update_x("wo", 1, 2)
            norm_mod(4, 1, 1, None, 13, A_IN)
            ffn(1, 1, 5)

            norm_mod(5, 2, 0, None, 13, A_IN)
            dve.wait_ge(S("sel"), 48)
            do(ts(gateb[:, :], gateb[:, :], 1.0 / CAP, None, ALU.mult), "gate_b")
            skip(["qk0", "qk1", "gt"])
            dve.wait_ge(S("softplus"), 1)
            G = lambda i: gts[:, i, :]
            do(dve.memset(G(6), 0.0))
            fence()
            do(dve.tensor_tensor_scan(G(2), G(1), G(6), 0.0, ALU.add, ALU.add))
            fence()
            do(stt(out=G(3), in0=G(0), scalar=CAP, in1=G(2), op0=ALU.mult, op1=ALU.add))
            fence()
            do(dve.tensor_tensor_scan(G(4), G(3), G(3), 0.0, ALU.max, ALU.max))
            fence()
            do(tt(G(5), G(2), G(4), ALU.subtract), "gates")
            fence("gates")
            dve.sem_inc(S("gates"), 1)
            skip(["mv0"])
            for c in range(2):
                wait_drained(dve, "acc", f"qk{c}")
            for f in range(NF):
                x, y = pl(2)[:, f, :], pl(12)[:, f, :]
                do(ts(y, x, V("ml_conv_w_2", 24 + f), V("ml_conv_b_2", f), ALU.mult, ALU.add))
                for tap, back in ((2, 1), (1, 2), (0, 3)):
                    fence()
                    do(stt(out=y[:, back:T], in0=x[:, 0:T - back], scalar=V("ml_conv_w_2", 8 * tap + f),
                           in1=y[:, back:T], op0=ALU.mult, op1=ALU.add), "ml_conv" if tap == 0 else "dve_step")
                if f == 3:
                    skip(["mv1"])
            skip(["o0", "o1"])
            ps = wait_filled(dve, "aux", "ut")
            cp(ucol, ps[:, 0:16]).then_inc(drained("aux", "ut"), 1)
            wait_drained(dve, "aux", "ut")

            def ml_out(h):
                ps = wait_filled(dve, "aux", f"nd{h}")
                wait_drained(dve, "aux", f"gb{h}")
                dn = ebuf[:, 2 + h % 2, :]
                do(stt(out=dn, in0=ps[:, T:2 * T], scalar=-1.0, in1=ebuf[:, h % 2, :], op0=ALU.mult, op1=ALU.max))
                fence()
                do(tt(dn, ps[:, T:2 * T], dn, ALU.max))
                fence()
                do(dve.reciprocal(dn, dn))
                fence()
                tt(pl(11)[:, h, :], ps[:, 0:T], dn, ALU.mult).then_inc(drained("aux", f"nd{h}"), 1)
                wait_drained(dve, "aux", f"nd{h}")
                dve.sem_inc(S("ml_y"), 1)

            for h in range(NF):
                ps = wait_filled(dve, "aux", f"gb{h}")
                dd = dbuf[:, h % 2, :]
                do(ts(dd[:, 0:T], ps[:, 0:T], ucol[:, h:h + 1], 0.0, ALU.subtract, ALU.max), "ml_dd")
                do(ts(dd[:, T:384], ps[:, P:T], ucol[:, NF + h:NF + h + 1], 0.0, ALU.subtract, ALU.max), "ml_dd")
                ps = wait_filled(dve, "aux", f"ms{h}")
                dve.wait_ge(S("ml_mask"), h + 1)
                if h >= 2:
                    wait_filled(dve, "aux", f"nd{h - 2}")
                stt(out=dbuf[:, 3 + h % 2, :], in0=ps[:, 0:384], scalar=64 ** -0.5, in1=dbuf[:, h % 2, :], op0=ALU.mult,
                    op1=ALU.mult).then_inc(drained("aux", f"ms{h}"), 1)
                wait_drained(dve, "aux", f"ms{h}")
                dve.sem_inc(S("ml_w"), 1)
                if h >= 1:
                    ml_out(h - 1)
            ml_out(NF - 1)
            head_scale(11, 12)
            fence()
            for c in range(2):
                wait_drained(dve, "acc", f"o{c}")
            for f in range(NF):
                y = pl(11)[:, f, :]
                do(stt(out=y, in0=y, scalar=V("ml_hn_w_2", f), in1=pl(5)[:, f, :], op0=ALU.mult, op1=ALU.mult))
                fence()
                to_input((plr(0)[:, f, :], plr(1)[:, f, :]), y, f)
            update_x("lo", 2, 2)
            norm_mod(6, 2, 1, None, 13, A_IN)
            ffn(2, 2, 5)
            norm_scale(7)
            for f in range(NF):
                do(stt(out=pl(0)[:, f, :], in0=X[:, f, :], scalar=V("final_w_2", f), in1=rs[:, :], op0=ALU.mult,
                       op1=ALU.mult), "y_out")

        @block.sync
        def _(sp):
            sp.dma_start(vec[:, :], d["vec"]).then_inc(S("vec_in"), 16)
            for j, (kind, _, srcs) in enumerate(slots):
                if j == 1:
                    sp.dma_start(cst[:, 0:C_BLK], d["cst"][:, 0:C_BLK]).then_inc(S("cst_in"), 16)
                if j == 2 * N_FIRST - 4:
                    sp.dma_start(X[:, :, :], d["x"]).then_inc(S("x_in"), 16)
                if j == 2 * N_FIRST + 3:
                    sp.dma_start(cst[:, C_BLK:], d["cst"][:, C_BLK:]).then_inc(S("cst_in"), 16)
                if j >= RING:
                    sp.wait_ge(*freed[j - RING])
                for rws, c0, n, ncols, src in srcs:
                    sp.dma_start(ring[0:rws, j % RING, c0:c0 + n * ncols].rearrange("p (k n) -> p k n", n=ncols), src)\
                        .then_inc(S(f"w_landed{j % RING}"), 16)
            for h in range(2):
                sp.wait_ge(S("y_out"), 4 * h + 4)
                sp.dma_start(d["out"][:, 4 * h:4 * h + 4, :], pl(0)[:, 4 * h:4 * h + 4, :]).then_inc(S("stored"), 16)
            sp.wait_ge(S("stored"), 32)


_VEC_NAMES = [n for n, _ in VECS]
_BIG = ["positions", "ada_w", "w_in", "ret_w_out", "conv_w_out", "mix_w_out", "ffn_w_gate", "ffn_w_up", "ffn_w_down",
        "ada_w_2", "rw_w_in_2", "rw_w2_2", "rw_a2_2", "rw_g2_2", "rw_w_out_2", "ml_w_in_2", "ml_b_i_2", "ml_b_f_2",
        "ml_w_out_2", "ffn_w_gu_2", "ffn_w_down_2"]


def kernel(**inputs):
    import concourse.bacc as bacc
    from concourse.bass_utils import run_bass_kernel_spmd

    nc = bacc.Bacc("TRN2", target_bir_lowering=False, num_devices=1)
    arrays = {n: np.ascontiguousarray(inputs[n]) for n in _BIG}
    arrays["x"] = np.ascontiguousarray(np.asarray(inputs["x"]).reshape(T, NF, P).transpose(2, 1, 0))
    arrays["vec"] = np.ascontiguousarray(
        np.concatenate([np.asarray(inputs[n]).reshape(-1, P) for n in _VEC_NAMES], 0).T)
    arrays["cst"], arrays["dec"], arrays["sel"] = shape_constants()
    d = {}
    for n, a in arrays.items():
        d[n] = nc.dram_tensor(f"in_{n}", a.shape, mybir.dt.from_np(a.dtype), kind="ExternalInput").ap()
    d["out"] = nc.dram_tensor("out_y", (P, NF, T), F32, kind="ExternalOutput").ap()
    build(nc, d)
    r = run_bass_kernel_spmd(nc, [{f"in_{n}": a for n, a in arrays.items()}], core_ids=[0])
    y = r.results[0]["out_y"]
    return np.ascontiguousarray(y.transpose(2, 1, 0)).reshape(1, T, D)
```
